# Optimizing a Trainium2 kernel written in Bass

```python
import math
import jax, jax.numpy as jnp
from jax import lax
import numpy as np

D_MODEL = 1024
BATCH = 1
SEQ = 128
DEPTH = 1
DEC_BATCH = 1
DEC_SEQ = 256
PAST_LEN = 128

GRID_W = 64
D_S5 = 3 * D_MODEL // 4
S5_GROUP = 16
S5_GROUPS = D_S5 // S5_GROUP
S5_STATE = 64
N_DIR = 2
DT_MIN = 1e-3
DT_MAX = 1e-1
D_FNET = D_MODEL - D_S5
FNET_GROUPS = 4
FNET_GROUP = D_FNET // FNET_GROUPS
N_BRANCH = 2
D_IN = D_S5 + D_FNET + N_BRANCH * D_MODEL
N_EXPERTS = 64
TOP_K = 6
N_EXPERT_GROUPS = 8
TOPK_GROUPS = 4
D_EXPERT = D_MODEL // 4
D_SHARED = D_MODEL // 4
ROUTED_SCALE = 2.5
N_MOD = 6
EPS = 1e-6

kernel_name = "s5_fnet_moe_prefix_diffusion_step"

def rms_norm(x, g):
    xf = x.astype(jnp.float32)
    y = xf * lax.rsqrt(jnp.mean(xf * xf, axis=-1, keepdims=True) + EPS) * g.astype(jnp.float32)
    return y.astype(x.dtype)

def grid_pos_embed(n_tokens, dtype):
    rows = n_tokens // GRID_W
    r, col = jnp.meshgrid(jnp.arange(rows, dtype=jnp.float32),
                          jnp.arange(GRID_W, dtype=jnp.float32), indexing="ij")
    quarter = D_MODEL // 4
    omega = 1.0 / (10000.0 ** (jnp.arange(quarter, dtype=jnp.float32) / quarter))

    def emb(pos):
        a = pos.reshape(-1)[:, None] * omega
        return jnp.concatenate([jnp.sin(a), jnp.cos(a)], axis=-1)

    return jnp.concatenate([emb(r), emb(col)], axis=-1).astype(dtype)

def adaln(cond, w_ada, b_ada):
    m = jax.nn.silu(cond) @ w_ada + b_ada
    m = m.reshape(cond.shape[:-1] + (N_MOD, D_MODEL))
    return [jnp.expand_dims(m[..., i, :], -2) for i in range(N_MOD)]

def _cmul(ar, ai, br, bi):
    return ar * br - ai * bi, ar * bi + ai * br

def _ssm_combine(e1, e2):
    a1r, a1i, b1r, b1i = e1
    a2r, a2i, b2r, b2i = e2
    ar, ai = _cmul(a1r, a1i, a2r, a2i)
    tr, ti = _cmul(a2r, a2i, b1r, b1i)
    return ar, ai, tr + b2r, ti + b2i

def s5_discretize(lam_re, lam_im, log_dt, b_re, b_im):
    lr = jnp.minimum(lam_re.astype(jnp.float32), -1e-4)
    li = lam_im.astype(jnp.float32)
    dt = jnp.exp(log_dt.astype(jnp.float32))[..., None]
    mag = jnp.exp(lr * dt)
    ar = mag * jnp.cos(li * dt)
    ai = mag * jnp.sin(li * dt)
    den = lr * lr + li * li
    nr = ar - 1.0
    qr = (nr * lr + ai * li) / den
    qi = (ai * lr - nr * li) / den
    br = b_re.astype(jnp.float32)
    bi = b_im.astype(jnp.float32)
    bbr = qr[..., None] * br - qi[..., None] * bi
    bbi = qr[..., None] * bi + qi[..., None] * br
    return ar, ai, bbr, bbi

def s5_scan(abar_r, abar_i, bu_r, bu_i, reverse):
    L = bu_r.shape[1]
    a_r = jnp.broadcast_to(abar_r, (1, L) + abar_r.shape)
    a_i = jnp.broadcast_to(abar_i, (1, L) + abar_i.shape)
    return lax.associative_scan(_ssm_combine, (a_r, a_i, bu_r, bu_i), reverse=reverse, axis=1)

def s5_branch(u, h0_r, h0_i, lam_re, lam_im, log_dt, b_re, b_im, c_re, c_im, d_skip, w_glu):
    Bn, L, _ = u.shape
    uf = u.astype(jnp.float32)
    ug = uf.reshape(Bn, L, S5_GROUPS, S5_GROUP)
    ar, ai, bbr, bbi = s5_discretize(lam_re, lam_im, log_dt, b_re, b_im)
    y = d_skip.astype(jnp.float32) * uf
    fin_r, fin_i = [], []
    for d in range(N_DIR):
        bu_r = jnp.einsum("gph,blgh->blgp", bbr[d], ug)
        bu_i = jnp.einsum("gph,blgh->blgp", bbi[d], ug)
        acr, aci, h_r, h_i = s5_scan(ar[d], ai[d], bu_r, bu_i, reverse=(d == 1))
        if h0_r is None:
            last = -1 if d == 0 else 0
            fin_r.append(h_r[:, last])
            fin_i.append(h_i[:, last])
        else:
            tr, ti = _cmul(acr, aci, h0_r[:, d, None].astype(jnp.float32), h0_i[:, d, None].astype(jnp.float32))
            h_r = h_r + tr
            h_i = h_i + ti
        read = (jnp.einsum("ghp,blgp->blgh", c_re[d].astype(jnp.float32), h_r)
                - jnp.einsum("ghp,blgp->blgh", c_im[d].astype(jnp.float32), h_i))
        y = y + read.reshape(Bn, L, D_S5)
    g = jax.nn.gelu(y)
    out = (g * jax.nn.sigmoid(g @ w_glu.astype(jnp.float32))).astype(u.dtype)
    if h0_r is None:
        return out, jnp.stack(fin_r, axis=1), jnp.stack(fin_i, axis=1)
    return out, None, None

def fourier_branch(z):
    Bn, L, _ = z.shape
    zf = z.astype(jnp.float32).reshape(Bn, L, FNET_GROUPS, FNET_GROUP)
    f = jnp.real(jnp.fft.fft2(zf, axes=(1, 3), norm="ortho"))
    return f.reshape(Bn, L, D_FNET).astype(z.dtype)

def moe(h, w_router, router_bias, w1, w3, w2, ws1, ws3, ws2):
    x = h.reshape(-1, D_MODEL)
    T = x.shape[0]
    scores = jax.nn.sigmoid((x @ w_router).astype(jnp.float32))
    biased = scores + router_bias.astype(jnp.float32)
    grp = biased.reshape(T, N_EXPERT_GROUPS, N_EXPERTS // N_EXPERT_GROUPS)
    grp_score = jnp.sum(lax.top_k(grp, 2)[0], axis=-1)
    _, grp_idx = lax.top_k(grp_score, TOPK_GROUPS)
    grp_mask = jnp.sum(jax.nn.one_hot(grp_idx, N_EXPERT_GROUPS, dtype=jnp.float32), axis=1)
    exp_mask = jnp.repeat(grp_mask, N_EXPERTS // N_EXPERT_GROUPS, axis=1)
    masked = jnp.where(exp_mask > 0, biased, -jnp.inf)
    _, idx = lax.top_k(masked, TOP_K)
    w = jnp.take_along_axis(scores, idx, axis=-1)
    w = w / jnp.sum(w, axis=-1, keepdims=True) * ROUTED_SCALE
    gates = jnp.sum(jax.nn.one_hot(idx, N_EXPERTS, dtype=jnp.float32) * w[..., None], axis=1)
    a = jnp.einsum("td,edf->tef", x, w1)
    b = jnp.einsum("td,edf->tef", x, w3)
    act = jax.nn.silu(a) * b * gates[:, :, None].astype(x.dtype)
    routed = jnp.einsum("tef,efd->td", act, w2)
    shared = (jax.nn.silu(x @ ws1) * (x @ ws3)) @ ws2
    return (routed + shared).reshape(h.shape).astype(h.dtype)

def trunk_layer(x, cond, h0_r, h0_i, p):
    sh1, sc1, g1, sh2, sc2, g2 = adaln(cond, p["w_ada"], p["b_ada"])
    h = rms_norm(x, p["norm1_g"]) * (1.0 + sc1) + sh1
    proj = h @ p["w_in"]
    u_s5 = proj[..., :D_S5]
    u_f = proj[..., D_S5:D_S5 + D_FNET]
    gl = jax.nn.sigmoid(proj[..., D_S5 + D_FNET:].astype(jnp.float32))
    gl = gl.reshape(gl.shape[:-1] + (N_BRANCH, D_MODEL))
    y_s5, st_r, st_i = s5_branch(u_s5, h0_r, h0_i, p["lam_re"], p["lam_im"], p["log_dt"],
                                 p["b_re"], p["b_im"], p["c_re"], p["c_im"], p["d_skip"], p["w_glu"])
    y_f = fourier_branch(u_f)
    merged = gl[..., 0, :] * (y_s5 @ p["w_proj_s5"]) + gl[..., 1, :] * (y_f @ p["w_proj_f"])
    x = x + g1 * (merged.astype(x.dtype) @ p["w_out"])
    h = rms_norm(x, p["norm2_g"]) * (1.0 + sc2) + sh2
    x = x + g2 * moe(h, p["w_router"], p["router_bias"], p["w1"], p["w3"], p["w2"],
                     p["ws1"], p["ws3"], p["ws2"])
    return x, st_r, st_i

def setup_inputs(seed: int = 0) -> dict:
    key = jax.random.key(seed)
    ks = jax.random.split(key, 32)
    f32 = jnp.float32
    nrm = lambda k, s, sc: jax.random.normal(k, s, f32) * sc
    n_idx = jnp.arange(S5_STATE, dtype=f32)
    lam_shape = (DEPTH, N_DIR, S5_GROUPS, S5_STATE)
    return {
        "x_prompt": nrm(ks[0], (BATCH, SEQ, D_MODEL), 1.0),
        "x_sample": nrm(ks[1], (DEC_BATCH, DEC_SEQ, D_MODEL), 1.0),
        "state_s5_re": nrm(ks[2], (DEC_BATCH, DEPTH, N_DIR, S5_GROUPS, S5_STATE), 0.5),
        "state_s5_im": nrm(ks[3], (DEC_BATCH, DEPTH, N_DIR, S5_GROUPS, S5_STATE), 0.5),
        "c": nrm(ks[4], (DEC_BATCH, D_MODEL), 1.0),
        "c_ctx": nrm(ks[5], (D_MODEL,), 1.0),
        "w_ada": nrm(ks[6], (DEPTH, D_MODEL, N_MOD * D_MODEL), 0.5 * D_MODEL ** -0.5),
        "b_ada": nrm(ks[7], (DEPTH, N_MOD * D_MODEL), 0.02),
        "norm1_g": 1.0 + nrm(ks[8], (DEPTH, D_MODEL), 0.02),
        "norm2_g": 1.0 + nrm(ks[9], (DEPTH, D_MODEL), 0.02),
        "w_in": nrm(ks[10], (DEPTH, D_MODEL, D_IN), D_MODEL ** -0.5),
        "lam_re": -0.5 + nrm(ks[11], lam_shape, 0.01),
        "lam_im": math.pi * n_idx + nrm(ks[12], lam_shape, 0.01),
        "log_dt": jax.random.uniform(ks[13], (DEPTH, N_DIR, S5_GROUPS), f32,
                                     math.log(DT_MIN), math.log(DT_MAX)),
        "b_re": nrm(ks[14], (DEPTH, N_DIR, S5_GROUPS, S5_STATE, S5_GROUP), (2 * S5_GROUP) ** -0.5),
        "b_im": nrm(ks[15], (DEPTH, N_DIR, S5_GROUPS, S5_STATE, S5_GROUP), (2 * S5_GROUP) ** -0.5),
        "c_re": nrm(ks[16], (DEPTH, N_DIR, S5_GROUPS, S5_GROUP, S5_STATE), S5_STATE ** -0.5),
        "c_im": nrm(ks[17], (DEPTH, N_DIR, S5_GROUPS, S5_GROUP, S5_STATE), S5_STATE ** -0.5),
        "d_skip": nrm(ks[18], (DEPTH, D_S5), 1.0),
        "w_glu": nrm(ks[19], (DEPTH, D_S5, D_S5), D_S5 ** -0.5),
        "w_proj_s5": nrm(ks[20], (DEPTH, D_S5, D_MODEL), D_S5 ** -0.5),
        "w_proj_f": nrm(ks[21], (DEPTH, D_FNET, D_MODEL), D_FNET ** -0.5),
        "w_out": nrm(ks[22], (DEPTH, D_MODEL, D_MODEL), D_MODEL ** -0.5),
        "w_router": nrm(ks[23], (DEPTH, D_MODEL, N_EXPERTS), D_MODEL ** -0.5),
        "router_bias": nrm(ks[24], (DEPTH, N_EXPERTS), 0.01),
        "w1": nrm(ks[25], (DEPTH, N_EXPERTS, D_MODEL, D_EXPERT), D_MODEL ** -0.5),
        "w3": nrm(ks[26], (DEPTH, N_EXPERTS, D_MODEL, D_EXPERT), D_MODEL ** -0.5),
        "w2": nrm(ks[27], (DEPTH, N_EXPERTS, D_EXPERT, D_MODEL), D_EXPERT ** -0.5),
        "ws1": nrm(ks[28], (DEPTH, D_MODEL, D_SHARED), D_MODEL ** -0.5),
        "ws3": nrm(ks[29], (DEPTH, D_MODEL, D_SHARED), D_MODEL ** -0.5),
        "ws2": nrm(ks[30], (DEPTH, D_SHARED, D_MODEL), D_SHARED ** -0.5),
        "final_norm_g": 1.0 + nrm(ks[31], (D_MODEL,), 0.02),
    }

def reference(x_prompt, x_sample, state_s5_re, state_s5_im, c, c_ctx, w_ada, b_ada, norm1_g, norm2_g,
              w_in, lam_re, lam_im, log_dt, b_re, b_im, c_re, c_im, d_skip, w_glu, w_proj_s5, w_proj_f,
              w_out, w_router, router_bias, w1, w3, w2, ws1, ws3, ws2, final_norm_g):
    ctx = x_prompt
    lat = x_sample + grid_pos_embed(x_sample.shape[1], x_sample.dtype)[None]
    new_re, new_im = [], []
    for l in range(DEPTH):
        p = dict(w_ada=w_ada[l], b_ada=b_ada[l], norm1_g=norm1_g[l], norm2_g=norm2_g[l], w_in=w_in[l],
                 lam_re=lam_re[l], lam_im=lam_im[l], log_dt=log_dt[l], b_re=b_re[l], b_im=b_im[l],
                 c_re=c_re[l], c_im=c_im[l], d_skip=d_skip[l], w_glu=w_glu[l], w_proj_s5=w_proj_s5[l],
                 w_proj_f=w_proj_f[l], w_out=w_out[l], w_router=w_router[l], router_bias=router_bias[l],
                 w1=w1[l], w3=w3[l], w2=w2[l], ws1=ws1[l], ws3=ws3[l], ws2=ws2[l])
        ctx, st_r, st_i = trunk_layer(ctx, c_ctx, None, None, p)
        lat, _, _ = trunk_layer(lat, c, state_s5_re[:, l], state_s5_im[:, l], p)
        new_re.append(st_r)
        new_im.append(st_i)
    y_prompt = rms_norm(ctx, final_norm_g)
    y_sample = rms_norm(lat, final_norm_g)
    new_state_re = jnp.stack(new_re, axis=1).astype(x_prompt.dtype)
    new_state_im = jnp.stack(new_im, axis=1).astype(x_prompt.dtype)
    return (y_prompt, y_sample, new_state_re, new_state_im)


_drawn_inputs = setup_inputs


def setup_inputs(seed=0):
    import zlib

    import numpy as np

    out = dict(_drawn_inputs(seed))
    spreads = {}
    factors = {'norm1_g': 3.414, 'lam_re': 4.499, 'final_norm_g': 2.885}
    for name, (base, spread) in spreads.items():
        noise = np.random.default_rng([zlib.crc32(name.encode()), seed]).standard_normal(out[name].shape)
        drawn = base * np.exp(spread * noise) if base else spread * noise
        out[name] = __import__('jax').numpy.asarray(drawn.astype(out[name].dtype))
    for name, factor in factors.items():
        out[name] = (out[name] * factor).astype(out[name].dtype)
    return out
```

```python
from contextlib import ExitStack

import numpy as np

import concourse.bass as bass
from concourse import mybir

F32 = mybir.dt.float32
I32 = mybir.dt.int32
ALU = mybir.AluOpType
ACT = mybir.ActivationFunctionType
AX_X = mybir.AxisListType.X

P = 128
D = 1024
CTX, LAT = 128, 256
TOK = CTX + LAT
NT = TOK // P
GRID_W = 64
KC = D // P
DS = 768
FT = DS // P
DF = 256
G, GH, NS = 48, 16, 64
Q = G // 2
DQ = 2 * Q
LC = 8
NC = TOK // LC
CC = CTX // LC
KW = (2 * LC - 1) * GH
E, TOPK, EG, EGS, EGK = 64, 6, 8, 8, 4
FE = 256
SL = 64
BATCH = 8
RING = 4
EPS = 1e-6
SCALE = 2.5
MAGIC = 1.5 * 2.0 ** 23
PI_A, PI_B, PI_C = 6.28125, 0.0019350051879882812, 3.0199157663701e-07
BIG = 1e30

C_ID, C_TRI, C_ONE, C_IOTA, C_M16, C_PAR, C_LOW = 0, 128, 256, 384, 448, 464, 496
N_CONST = 560
F_CTX, F_LAT, F_BC, F_BS = 0, 256, 1280, 1408
N_DFT = 1536


OUTS = dict(y_prompt=(1, CTX, D), y_sample=(1, LAT, D), st_re=(1, 1, 2, G, NS), st_im=(1, 1, 2, G, NS))


def shape_constants():
    p = np.arange(P)
    k = np.zeros((P, N_CONST), np.float32)
    k[:, C_ID:C_ID + P] = np.eye(P)
    k[:, C_TRI:C_TRI + P] = p[:, None] < p[None, :]
    k[:, C_ONE:C_ONE + P] = 1.0
    k[:, C_IOTA:C_IOTA + 64] = np.arange(64)
    k[:, C_M16:C_M16 + GH] = (p[:, None] % GH) == np.arange(GH)
    k[:, C_PAR:C_PAR + 32] = (p[:, None] // NS) == (np.arange(32) // GH)
    k[:, C_LOW:C_LOW + 64] = (np.arange(8)[:, None] > np.arange(8)[None, :]).reshape(-1)
    f = np.zeros((P, N_DFT))

    def dft(n):
        a = 2 * np.pi * (np.outer(np.arange(n), np.arange(n)) % n) / n
        return np.cos(a) / np.sqrt(n), np.sin(a) / np.sqrt(n)

    c, s = dft(CTX)
    f[:, F_CTX:F_CTX + 256] = np.concatenate([c, s], 1)
    c, s = dft(LAT)
    f[:, F_LAT:F_LAT + 1024] = np.concatenate([c, s], 1).reshape(2, P, 512).transpose(1, 0, 2).reshape(P, 1024)
    c, s = dft(64)
    f[:, F_BC:F_BC + P] = np.kron(np.eye(2), c)
    f[:, F_BS:F_BS + P] = -np.kron(np.eye(2), s)
    quarter = D // 4
    omega = (1.0 / (10000.0 ** (np.arange(quarter, dtype=np.float32) / quarter))).astype(np.float32)

    def emb(pos):
        a = pos.astype(np.float32)[:, None] * omega
        return np.concatenate([np.sin(a), np.cos(a)], -1)

    t = np.arange(LAT)
    pos = np.concatenate([emb(t // GRID_W), emb(t % GRID_W)], -1).astype(np.float32)
    return k, f.astype(np.float32), pos


def build(nc, i, o):
    with ExitStack() as ctx:
        def sem(name):
            return ctx.enter_context(nc.semaphore(name))

        sb = ctx.enter_context(nc.sbuf_tensor("sb", [P, 53184], F32))
        bank = [ctx.enter_context(nc.psum_tensor(f"bank{n}", [P, 512], F32)) for n in range(8)]

        top = [0]

        def region(n):
            top[0] += n
            return top[0] - n

        def at(base, n, rows=slice(0, P)):
            return sb[rows, base:base + n]

        o_const, o_mod, o_misc = region(N_CONST), region(96), region(528)
        o_A, o_B = region(12288), region(12288)
        o_V, o_W, o_H, o_U, o_T = region(6144), region(10240), region(3072), region(2304), region(2048)
        o_K, o_S, o_Z, o_ch = region(1440), region(768), region(768), region(576)
        assert top[0] <= 53184, top[0]

        const = at(o_const, N_CONST)
        ident = const[:, C_ID:C_ID + P]
        mod = at(o_mod, 96).rearrange("p (r m c) -> p r m c", r=2, m=6)
        misc = at(o_misc, 528)
        ada_dram = nc.dram_tensor("ada_dram", [2, 6 * D], F32).ap()


        chan = at(o_ch, 576).rearrange("p (a n) -> p a n", n=DQ)
        a_pow = [chan[:, 2 * k:2 * k + 2, :] for k in range(3)]
        Arr, Aii = chan[:, 6:8, :], chan[:, 8:10, :]
        h0 = chan[:, 10:12, :]

        BP = at(o_A, 12288).rearrange("p (r n s h) -> p r n s h", r=2, n=DQ, h=GH)
        CP = at(o_B, 12288).rearrange("p (r n s h) -> p r n s h", r=2, n=DQ, h=GH)
        KK = at(o_K, FT * KW).rearrange("p (f k) -> p f k", f=FT)
        hT = at(o_H, KC * TOK).rearrange("p (c t) -> p c t", c=KC)
        uT = at(o_U, FT * TOK).rearrange("p (f t) -> p f t", f=FT)
        Z = at(o_Z, 768).rearrange("p (j n) -> p j n", j=NT)

        NR = 5
        ring = at(o_W, NR * 2048).rearrange("p (s n) -> p s n", s=NR)
        items = [("ada", 0, c) for c in range(KC + 1)] + [("in", 0, c) for c in range(4)]
        items += [("ada", b, c) for b in (1, 2) for c in range(KC + 1)]
        where = {it: n for n, it in enumerate(items)}
        ring_in = [sem(f"ring_in{n}") for n in range(NR)]
        ring_used = sem("ring_used")
        s_const, s_cond, s_rows, s_c, s_b, s_dg = [sem(n) for n in ("s_const", "s_cond", "s_rows", "s_c", "s_b", "s_dg")]
        s_x = [sem(f"s_x{n}") for n in range(3)]
        s_pos = [sem(f"s_pos{n}") for n in range(2)]
        s_csil, ada_row, ada_out, s_mod, s_gs1 = [sem(n) for n in (
            "s_csil", "ada_row", "ada_out", "s_mod", "s_gs1")]
        prm_act, prm_dve, row_dve, row_T, chan_ok = [sem(n) for n in ("prm_act", "prm_dve", "row_dve", "row_T", "chan_ok")]
        ct_T, ct_ok, cpad_ok, bp_ok, bp_step, cp_step, cp_ok = [sem(n) for n in (
            "ct_T", "ct_ok", "cpad_ok", "bp_ok", "bp_step", "cp_step", "cp_ok")]
        nrm_xt, nrm_sq, nrm_ms, nrm_rt, nrm_xn, nrm_dve, xT_mm, hT_ok = [sem(n) for n in (
            "nrm_xt", "nrm_sq", "nrm_ms", "nrm_rt", "nrm_xn", "nrm_dve", "xT_mm", "hT_ok")]
        u_mm, u_ok, z_mm, z_ok, kk_mm, kk_act, kk_ok, zero_ok = [sem(n) for n in (
            "u_mm", "u_ok", "z_mm", "z_ok", "kk_mm", "kk_act", "kk_ok", "zero_ok")]

        cond = misc[:, 0:16].rearrange("p (r c) -> p r c", r=2)
        g1n, g2n = misc[:, 16:24], misc[:, 24:32]
        gs1 = misc[:, 32:48].rearrange("p (r c) -> p r c", r=2)
        gs2 = misc[:, 48:64].rearrange("p (r c) -> p r c", r=2)
        dsk = misc[:, 64:70]
        nst = misc[:, 72:96]
        csil = misc[:, 128:384].rearrange("p (c m) -> p c m", m=32)
        tmpc = misc[:, 384:480].rearrange("p (a n) -> p a n", n=DQ)

        rows = at(o_A, 24 * P, slice(0, DQ)).rearrange("p (a n) -> p a n", n=P)
        (LR, LI, XR, TH, KQ, RR, RH, SN, SH, CS, MG, DEN, NRr, T1, T2) = [rows[:, n] for n in range(6, 21)]
        AR, AI, QR, QI, H0R, H0I = [rows[:, n] for n in range(6)]
        LD, DT = rows[:, 21, 0:2], rows[:, 21, 4:6]
        CL = at(o_A + 3072, 12 * P).rearrange("p (f n) -> p f n", n=P)
        BL = at(o_V, 1536).rearrange("p (r n h) -> p r n h", r=2, h=GH)
        CT = at(o_V + 1536, 1536).rearrange("p (r n h) -> p r n h", r=2, h=GH)
        Cpad = at(o_V + 3072, 3072).rearrange("p (r n m) -> p r n m", r=2, m=32)
        q_ch = at(o_U + 1536, 96).rearrange("p (r n) -> p r n", r=2)
        bp_tmp = at(o_U, 1536)
        cp_tmp = at(o_S, 768)
        xbuf = at(o_T, 2048).rearrange("p (b n) -> p b n", b=2)
        xsq = at(o_K, D)
        ada_sb = [at(o_Z, 512), at(o_T, 512), at(o_T + 512, 512)]

        def src_cond(name):
            v = i[name]
            v = v.rearrange("(a d) -> a d", a=1) if len(v.shape) == 1 else v
            return v.rearrange("a (p c) -> p (a c)", p=P)

        with nc.Block() as block:
            @block.sync
            def _(sp):
                def load(n):
                    kind, b, c = items[n]
                    if n >= NR:
                        sp.wait_ge(ring_used, n - NR + 1)
                    dst = ring[:, n % NR, :]
                    if kind == "ada" and c < KC:
                        src = i["w_ada"][0].rearrange("(p c) n -> p c n", c=KC)[:, c, 2048 * b:2048 * (b + 1)]
                    elif kind == "ada":
                        dst, src = ring[0:1, n % NR, :], i["b_ada"][:, 2048 * b:2048 * (b + 1)]
                    else:
                        dst = dst.rearrange("p (c n) -> p c n", c=2)
                        src = i["w_in"][0].rearrange("(p c) n -> p c n", c=KC)[:, 2 * c:2 * c + 2, 0:1024]
                    sp.dma_start(dst, src).then_inc(ring_in[n % NR], 16)

                sp.dma_start(const, i["k_const"]).then_inc(s_const, 16)
                sp.dma_start(cond[:, 0], src_cond("c_ctx")).then_inc(s_cond, 16)
                sp.dma_start(cond[:, 1], src_cond("c")).then_inc(s_cond, 16)
                sp.dma_start(LR, i["lam_re"][0].rearrange("d (q a) n -> (d q) (a n)", a=2)).then_inc(s_rows, 16)
                sp.dma_start(LI, i["lam_im"][0].rearrange("d (q a) n -> (d q) (a n)", a=2)).then_inc(s_rows, 16)
                sp.dma_start(LD, i["log_dt"][0].rearrange("d (q a) -> (d q) a", a=2)).then_inc(s_rows, 16)
                sp.dma_start(H0R, i["state_s5_re"][0, 0].rearrange("d (q a) n -> (d q) (a n)", a=2)).then_inc(s_rows, 16)
                sp.dma_start(H0I, i["state_s5_im"][0, 0].rearrange("d (q a) n -> (d q) (a n)", a=2)).then_inc(s_rows, 16)
                for n in range(NR):
                    load(n)
                for n in range(NR, len(items)):
                    load(n)

            @block.gpsimd
            def _(pool):
                for r, name in enumerate(("c_re", "c_im")):
                    v = i[name][0].rearrange("d (f q a) h n -> q a h (d f) n", q=4, a=2)
                    for q in range(4):
                        for a in range(2):
                            pool.dma_start(CL[(r * 4 + q) * GH:(r * 4 + q + 1) * GH, :, a * NS:(a + 1) * NS],
                                           v[q, a]).then_inc(s_c, 16)
                for r, name in enumerate(("b_re", "b_im")):
                    pool.dma_start(BL[:, r], i[name][0].rearrange("d (q a) n h -> (a n) (d q) h", a=2)).then_inc(s_b, 16)
                pool.dma_start(g1n, i["norm1_g"][0].rearrange("(p c) -> p c", c=KC)).then_inc(s_dg, 16)
                pool.dma_start(g2n, i["norm2_g"][0].rearrange("(p c) -> p c", c=KC)).then_inc(s_dg, 16)
                pool.dma_start(dsk, i["d_skip"][0].rearrange("(f p) -> p f", p=P),
                               allow_slow_non_contiguous=True).then_inc(s_dg, 16)
                pool.wait_ge(ct_ok, 3)
                pool.wait_ge(chan_ok, 1)
                steps = 0
                for m in (0, 1, 2, 4):
                    av = a_pow[{0: 0, 1: 0, 2: 1, 4: 2}[m]]
                    w = max(m, 1)
                    for d in range(2):
                        for half in range(2):
                            qs = slice(d * Q + half * 12, d * Q + half * 12 + 12)
                            if m == 0:
                                src = [CT[:, r, qs, :].unsqueeze(2) for r in range(2)]
                                dst = slice(0, 1) if d == 0 else slice(7, 8)
                            elif d == 0:
                                src = [CP[:, r, qs, 0:w, :] for r in range(2)]
                                dst = slice(w, 2 * w)
                            else:
                                src = [CP[:, r, qs, 8 - w:8, :] for r in range(2)]
                                dst = slice(8 - 2 * w, 8 - w)
                            flat = lambda v: v.rearrange("p n s h -> p n (s h)")
                            src = [flat(v) for v in src]
                            outs = [flat(CP[:, r, qs, dst, :]) for r in range(2)]
                            t = cp_tmp[:, 0:12 * w * GH].rearrange("p (n k) -> p n k", n=12)
                            ar, ai = [av[:, r, qs].unsqueeze(2).to_broadcast([P, 12, w * GH]) for r in range(2)]
                            for (x1, x2, op, dest) in ((0, 1, ALU.add, outs[0]), (1, 0, ALU.subtract, outs[1])):
                                if steps:
                                    pool.wait_ge(cp_step, steps)
                                pool.tensor_tensor(t, src[x2], ai, ALU.mult)
                                pool.tensor_tensor(dest, src[x1], ar, ALU.mult).then_inc(cp_step, 1)
                                steps += 1
                                pool.wait_ge(cp_step, steps)
                                pool.tensor_tensor(dest, dest, t, op).then_inc(cp_step, 1)
                                steps += 1

            @block.scalar
            def _(act):
                def x_tile(j):
                    if j == 2:
                        act.wait_ge(xT_mm, 2)
                    src = i["x_prompt"][0] if j == 0 else i["x_sample"][0, (j - 1) * P:j * P, :]
                    act.dma_start(xbuf[:, j % 2, :], src).then_inc(s_x[j], 16)

                def squares(j):
                    act.wait_ge(nrm_xt, j + 1)
                    if j:
                        act.wait_ge(nrm_sq, j)
                    nc.scalar.activation(xsq, xbuf[:, j % 2, :], ACT.Square, accum_out=nst[:, j:j + 1]).then_inc(nrm_sq, 1)
                    act.wait_ge(nrm_ms, j + 1)
                    nc.scalar.activation(nst[:, 8 + j:9 + j], nst[:, 4 + j:5 + j], ACT.Sqrt).then_inc(nrm_rt, 1)

                x_tile(0)
                x_tile(1)
                act.dma_start(at(o_H, D), i["k_pos"][0:P, :]).then_inc(s_pos[0], 16)
                act.dma_start(at(o_H + D, D), i["k_pos"][P:2 * P, :]).then_inc(s_pos[1], 16)
                act.wait_ge(zero_ok, 1)
                act.wait_ge(s_cond, 32)
                for r in range(2):
                    nc.scalar.activation(csil[:, :, r], cond[:, r], ACT.Silu).then_inc(s_csil, 1)
                act.wait_ge(s_rows, 80)
                nc.scalar.activation(DT, LD, ACT.Exp).then_inc(prm_act, 1)
                act.wait_ge(prm_dve, 1)
                nc.scalar.activation(MG, XR, ACT.Exp).then_inc(prm_act, 1)
                act.wait_ge(prm_dve, 2)
                nc.scalar.activation(SN, RR, ACT.Sin).then_inc(prm_act, 1)
                nc.scalar.activation(SH, RH, ACT.Sin).then_inc(prm_act, 1)
                squares(0)
                squares(1)
                for f in range(3):
                    act.wait_ge(ct_T, f + 1)
                    for k in range(4):
                        for r in range(2):
                            n = (4 * f + k) * 4
                            ins = nc.scalar.activation(
                                CT[:, r, n:n + 4, :].rearrange("p n h -> p (n h)"),
                                bank[f][:, k * P + r * 64:k * P + r * 64 + 64], ACT.Copy, scale=1.0 if r == 0 else -1.0)
                    ins.then_inc(ct_ok, 1)

                def ada_rows(b):
                    act.wait_ge(ring_used, where["ada", b, KC] + 1)
                    nc.scalar.activation(ada_sb[b], bank[0][:, :], ACT.Copy).then_inc(ada_row, 1)
                    act.wait_ge(ada_row, b + 1)
                    for j in range(4):
                        n = 2048 * b + 512 * j
                        act.dma_start(ada_dram[:, n:n + 512], ada_sb[b][32 * j:32 * j + 2, :]).then_inc(ada_out, 16)

                ada_rows(0)
                act.wait_ge(ada_out, 64)
                for r in range(2):
                    act.dma_start(mod[:, r, 0:2, :], ada_dram[r, 0:2 * D].rearrange("(m p c) -> p m c", m=2, c=KC)
                                  ).then_inc(s_mod, 16)
                x_tile(2)
                squares(2)
                act.wait_ge(s_gs1, 1)
                for j in range(NT):
                    r = 0 if j == 0 else 1
                    for h in range(2):
                        act.wait_ge(xT_mm, 2 * j + h + 1)
                        for c in range(4):
                            cc = 4 * h + c
                            ins = nc.scalar.activation(hT[:, cc, j * P:(j + 1) * P], bank[1 + h][:, c * P:(c + 1) * P],
                                                       ACT.Identity, scale=gs1[:, r, cc:cc + 1], bias=mod[:, r, 0, cc:cc + 1])
                        ins.then_inc(hT_ok, 1)
                act.wait_ge(bp_ok, 2)
                for f in range(FT):
                    act.wait_ge(u_mm, f + 1)
                    nc.scalar.activation(uT[:, f, :], bank[3 + f % 2][:, 0:TOK], ACT.Copy).then_inc(u_ok, 1)
                for j in range(NT):
                    if j < NT - 1:
                        act.wait_ge(z_mm, j + 1)
                    else:
                        act.wait_ge(ring_used, KC + 1 + 4)
                    nc.scalar.activation(Z[:, j, :], bank[5 + j % 2][:, 0:DF], ACT.Copy).then_inc(z_ok, 1)
                ada_rows(1)
                ada_rows(2)
                for f in range(FT):
                    act.wait_ge(kk_mm, f + 1)
                    w = (LC - 1) * GH
                    nc.scalar.activation(KK[:, f, 0:w], bank[6 + f % 2][:, 0:w], ACT.Copy)
                    nc.scalar.activation(KK[:, f, w + GH:KW], bank[6 + f % 2][:, w + GH:KW], ACT.Copy).then_inc(kk_act, 1)
                act.wait_ge(ada_out, 192)

            @block.tensor
            def _(pe):
                pe.wait_ge(s_const, 16)
                pe.wait_ge(s_c, 256)
                for f in range(3):
                    for k in range(4):
                        ins = nc.tensor.transpose(bank[f][:, k * P:(k + 1) * P], CL[:, 4 * f + k, :], ident)
                    ins.then_inc(ct_T, 1)
                pe.wait_ge(row_dve, 1)
                for k in range(6):
                    ins = nc.tensor.transpose(bank[7][:, k * DQ:(k + 1) * DQ], rows[:, k], ident[0:DQ, 0:DQ])
                ins.then_inc(row_T, 1)

                def arrived(it):
                    n = where[it]
                    pe.wait_ge(ring_in[n % NR], 16 * (n // NR + 1))
                    return ring[:, n % NR, :]

                def ada(b):
                    if b == 0:
                        pe.wait_ge(ct_ok, 1)
                    else:
                        pe.wait_ge(ada_row, b)
                    for c in range(KC + 1):
                        w = arrived(("ada", b, c))
                        if c == 0 and b == 0:
                            pe.wait_ge(s_csil, 2)
                        for j in range(4):
                            lhs = csil[:, c, :] if c < KC else const[0:1, C_ONE:C_ONE + 32]
                            rhs = w[:, 512 * j:512 * j + 512] if c < KC else w[0:1, 512 * j:512 * j + 512]
                            ins = nc.tensor.matmul(bank[0][32 * j:32 * j + 32, :], lhs, rhs, start=c == 0, stop=c == KC)
                        ins.then_inc(ring_used, 1)

                pe.wait_ge(chan_ok, 1)
                ada(0)
                for j in range(NT):
                    pe.wait_ge(nrm_xn, j + 1)
                    for h in range(2):
                        if j == 0:
                            pe.wait_ge(ct_ok, 2 + h)
                        else:
                            pe.wait_ge(hT_ok, 2 * (j - 1) + h + 1)
                        for c in range(4):
                            ins = nc.tensor.transpose(bank[1 + h][:, c * P:(c + 1) * P],
                                                      xbuf[:, j % 2, 4 * h + c:D:KC], ident)
                        ins.then_inc(xT_mm, 1)
                w_a = [arrived(("in", 0, c // 2)).rearrange("p (c n) -> p c n", c=2)[:, c % 2] for c in range(KC)]
                pe.wait_ge(hT_ok, 6)
                for f in range(FT):
                    if f >= 2:
                        pe.wait_ge(u_ok, f - 1)
                    for c in range(KC):
                        ins = nc.tensor.matmul(bank[3 + f % 2][:, 0:TOK], w_a[c][:, f * P:(f + 1) * P], hT[:, c, :],
                                               start=c == 0, stop=c == KC - 1)
                    ins.then_inc(u_mm, 1)
                for j in range(NT):
                    if j >= 2:
                        pe.wait_ge(z_ok, j - 1)
                    for c in range(KC):
                        ins = nc.tensor.matmul(bank[5 + j % 2][:, 0:DF], hT[:, c, j * P:(j + 1) * P], w_a[c][:, DS:DS + DF],
                                               start=c == 0, stop=c == KC - 1)
                    if j < NT - 1:
                        ins.then_inc(z_mm, 1)
                    else:
                        ins.then_inc(ring_used, 4)
                ada(1)
                ada(2)
                pe.wait_ge(cpad_ok, 2)
                pe.wait_ge(bp_ok, 2)
                for f in range(FT):
                    if f >= 2:
                        pe.wait_ge(kk_ok, f - 1)
                    elif f == 0:
                        pe.wait_ge(z_ok, 3)
                    for q in range(4):
                        for n, (d, r) in enumerate(((0, 0), (0, 1), (1, 0), (1, 1))):
                            dq = d * Q + 4 * f + q
                            c0 = 0 if d == 0 else (LC - 1) * GH
                            ins = nc.tensor.matmul(bank[6 + f % 2][32 * q:32 * q + 32, c0:c0 + P], Cpad[:, r, dq, :],
                                                   BP[:, r, dq].rearrange("p s h -> p (s h)"),
                                                   start=n == 0, stop=n == 3, skip_group_check=True)
                    ins.then_inc(kk_mm, 1)

            @block.vector
            def _(dve):
                dve_step = sem("dve_step1")
                n_step = [0]

                def step(ins):
                    n_step[0] += 1
                    ins.then_inc(dve_step, 1)
                    dve.wait_ge(dve_step, n_step[0])

                tt = nc.vector.tensor_tensor
                ts = nc.vector.tensor_scalar
                stt = nc.vector.scalar_tensor_tensor
                nc.vector.memset(csil[:, :, :], 0.0).then_inc(zero_ok, 1)
                dve.wait_ge(s_rows, 80)
                step(ts(LR, LR, -1e-4, None, ALU.min))
                dve.wait_ge(prm_act, 1)
                for a in range(2):
                    cols = slice(a * NS, (a + 1) * NS)
                    ts(TH[:, cols], LI[:, cols], DT[:, a:a + 1], None, ALU.mult)
                    ins = ts(XR[:, cols], LR[:, cols], DT[:, a:a + 1], None, ALU.mult)
                ins.then_inc(prm_dve, 1)
                dve.wait_ge(prm_dve, 1)
                step(ts(KQ, TH, 1.0 / (2 * np.pi), MAGIC, ALU.mult, ALU.add))
                step(ts(KQ, KQ, MAGIC, None, ALU.subtract))
                step(stt(out=RR, in0=KQ, scalar=-PI_A, in1=TH, op0=ALU.mult, op1=ALU.add))
                step(stt(out=RR, in0=KQ, scalar=-PI_B, in1=RR, op0=ALU.mult, op1=ALU.add))
                step(stt(out=RR, in0=KQ, scalar=-PI_C, in1=RR, op0=ALU.mult, op1=ALU.add))
                step(ts(RR, RR, 3.1415925, -3.1415925, ALU.min, ALU.max))
                ts(RH, RR, 0.5, None, ALU.mult).then_inc(prm_dve, 1)
                tt(DEN, LR, LR, ALU.mult)
                step(tt(T1, LI, LI, ALU.mult))
                step(tt(DEN, DEN, T1, ALU.add))
                step(nc.vector.reciprocal(DEN, DEN))
                dve.wait_ge(prm_act, 4)
                step(tt(CS, SH, SH, ALU.mult))
                step(ts(CS, CS, -2.0, 1.0, ALU.mult, ALU.add))
                tt(AI, MG, SN, ALU.mult)
                step(tt(AR, MG, CS, ALU.mult))
                step(ts(NRr, AR, 1.0, None, ALU.subtract))
                tt(T1, AI, LI, ALU.mult)
                step(tt(T2, NRr, LR, ALU.mult))
                step(tt(T1, T1, T2, ALU.add))
                step(tt(QR, T1, DEN, ALU.mult))
                tt(T1, AI, LR, ALU.mult)
                step(tt(T2, NRr, LI, ALU.mult))
                step(tt(T1, T1, T2, ALU.subtract))
                tt(QI, T1, DEN, ALU.mult).then_inc(row_dve, 1)
                dve.wait_ge(row_T, 1)
                rt = bank[7][:, 0:6 * DQ].rearrange("p (a n) -> p a n", n=DQ)
                nc.vector.tensor_copy(a_pow[0], rt[:, 0:2])
                nc.vector.tensor_copy(q_ch, rt[:, 2:4])
                step(nc.vector.tensor_copy(h0, rt[:, 4:6]))
                for k in range(3):
                    x = a_pow[k]
                    tt(tmpc[:, 0], x[:, 0], x[:, 0], ALU.mult)
                    tt(tmpc[:, 1], x[:, 1], x[:, 1], ALU.mult)
                    if k < 2:
                        step(stt(out=a_pow[k + 1][:, 1], in0=x[:, 0], scalar=2.0, in1=x[:, 1], op0=ALU.mult, op1=ALU.mult))
                        step(tt(a_pow[k + 1][:, 0], tmpc[:, 0], tmpc[:, 1], ALU.subtract))
                    else:
                        stt(out=Aii[:, 0], in0=x[:, 0], scalar=-2.0, in1=x[:, 1], op0=ALU.mult, op1=ALU.mult)
                        step(stt(out=Aii[:, 1], in0=x[:, 0], scalar=2.0, in1=x[:, 1], op0=ALU.mult, op1=ALU.mult))
                        tt(Arr[:, 0], tmpc[:, 0], tmpc[:, 1], ALU.subtract)
                        step(tt(Arr[:, 1], tmpc[:, 0], tmpc[:, 1], ALU.subtract))
                nc.vector.tensor_copy(tmpc[:, 0, 0:1], tmpc[:, 0, 1:2]).then_inc(chan_ok, 1)

                def norm(j):
                    dve.wait_ge(s_x[j], 16)
                    x = xbuf[:, j % 2, :]
                    if j:
                        dve.wait_ge(s_pos[j - 1], 16)
                        tt(x, x, at(o_H + (j - 1) * D, D), ALU.add).then_inc(nrm_xt, 1)
                    else:
                        ts(nst[:, 23:24], x[:, 0:1], 1.0, None, ALU.mult).then_inc(nrm_xt, 1)
                    dve.wait_ge(nrm_sq, j + 1)
                    ts(nst[:, 4 + j:5 + j], nst[:, j:j + 1], 1.0 / D, EPS, ALU.mult, ALU.add).then_inc(nrm_ms, 1)
                    dve.wait_ge(nrm_rt, j + 1)
                    step(nc.vector.reciprocal(nst[:, 12 + j:13 + j], nst[:, 8 + j:9 + j]))
                    ts(x, x, nst[:, 12 + j:13 + j], None, ALU.mult).then_inc(nrm_xn, 1)

                norm(0)
                norm(1)
                dve.wait_ge(ct_ok, 3)
                for r in range(2):
                    tt(Cpad[:, r].rearrange("p n (a h) -> p n a h", a=2),
                       CT[:, r].unsqueeze(2).to_broadcast([P, DQ, 2, GH]),
                       const[:, C_PAR:C_PAR + 32].rearrange("p (a h) -> p a h", a=2).unsqueeze(1).to_broadcast([P, DQ, 2, GH]),
                       ALU.mult).then_inc(cpad_ok, 1)
                dve.wait_ge(s_b, 32)
                flat = lambda v: v.rearrange("p n s h -> p n (s h)")

                def bp_level(d, m):
                    w = max(m, 1)
                    qs = slice(d * Q, (d + 1) * Q)
                    if m == 0:
                        src = [BL[:, r, qs, :] for r in range(2)]
                        dst = slice(7, 8) if d == 0 else slice(0, 1)
                        av = q_ch
                    else:
                        av = a_pow[{1: 0, 2: 1, 4: 2}[m]]
                        src = [flat(BP[:, r, qs, 8 - w:8, :] if d == 0 else BP[:, r, qs, 0:w, :]) for r in range(2)]
                        dst = slice(8 - 2 * w, 8 - w) if d == 0 else slice(w, 2 * w)
                    outs = [flat(BP[:, r, qs, dst, :]) for r in range(2)]
                    t = bp_tmp[:, 0:Q * w * GH].rearrange("p (n k) -> p n k", n=Q)
                    ar, ai = [av[:, r, qs].unsqueeze(2).to_broadcast([P, Q, w * GH]) for r in range(2)]
                    for (x1, x2, op, dest) in ((0, 1, ALU.subtract, outs[0]), (1, 0, ALU.add, outs[1])):
                        tt(t, src[x2], ai, ALU.mult)
                        step(tt(dest, src[x1], ar, ALU.mult))
                        step(tt(dest, dest, t, op))

                for m in (0, 1, 2, 4):
                    bp_level(0, m)
                norm(2)
                dve.wait_ge(s_mod, 32)
                dve.wait_ge(s_dg, 48)
                for r in range(2):
                    ins = stt(out=gs1[:, r], in0=mod[:, r, 1, :], scalar=1.0, in1=g1n, op0=ALU.add, op1=ALU.mult)
                ins.then_inc(s_gs1, 1)
                for m in (0, 1, 2, 4):
                    bp_level(1, m)
                nc.vector.tensor_copy(tmpc[:, 0, 0:1], tmpc[:, 0, 1:2]).then_inc(bp_ok, 2)
                for f in range(FT):
                    dve.wait_ge(kk_act, f + 1)
                    w = (LC - 1) * GH
                    stt(out=KK[:, f, w:w + GH], in0=const[:, C_M16:C_M16 + GH], scalar=dsk[:, f:f + 1],
                        in1=bank[6 + f % 2][:, w:w + GH], op0=ALU.mult, op1=ALU.add).then_inc(kk_ok, 1)

        Uc = at(o_V, LC * DS, slice(0, NC))
        U = at(o_U, G * NC).rearrange("p (g k) -> p g k", g=G)
        V = at(o_V, 2 * DQ * NC).rearrange("p (r n k) -> p r n k", r=2, n=DQ)
        GLT = at(o_A, 16 * TOK).rearrange("p (m t) -> p m t", m=16)
        Sin = at(o_A + 6144, 2 * DQ * NC).rearrange("p (r n k) -> p r n k", r=2, n=DQ)
        Srev = at(o_S, 768).rearrange("p (b r n k) -> p b r n k", b=2, r=2, n=4)
        BT = at(o_T, 2048).rearrange("p (s x n) -> p s x n", s=4, x=4)
        Tt = at(o_T, 2048).rearrange("p (b g t h) -> p b g t h", b=2, g=8, h=GH)
        Yc = at(o_V, LC * DS, slice(0, NC)).rearrange("p (t f) -> p t f", t=LC)
        fin = misc[:, 128:224].rearrange("p (r n) -> p r n", r=2)
        fin_rows = [at(o_ch + P * r, P, slice(0, DQ)) for r in range(2)]
        t1, t2 = [misc[:, 224 + 96 * k:320 + 96 * k].rearrange("p (r n) -> p r n", r=2) for k in range(2)]
        t3 = misc[:, 416:512].rearrange("p (r n) -> p r n", r=2)
        gate_in = [sem(f"gate_in{n}") for n in range(NR)]
        uc_T, uc_ok, u2_T, u2_ok, bt_T, bt_ok, v_mm, v_ok, scan_ok, fin_ok, fin_T, fin_row, st_out = [sem(n) for n in (
            "uc_T", "uc_ok", "u2_T", "u2_ok", "bt_T", "bt_ok", "v_mm", "v_ok", "scan_ok", "fin_ok", "fin_T", "fin_row", "st_out")]
        gl_mm, gl_ok, t_T, t_ok, srev_ok, y_mm, y_ok = [sem(n) for n in (
            "gl_mm", "gl_ok", "t_T", "t_ok", "srev_ok", "y_mm", "y_ok")]
        w_glu = at(o_W, FT * DS).rearrange("p (k n) -> p k n", k=FT)
        w_p5 = at(o_W + FT * DS, 5 * D).rearrange("p (k n) -> p k n", k=5)
        glu_in, p5_in = sem("glu_in"), sem("p5_in")
        NUC = LC * FT // 4

        def uc_copy(b):
            f, half = divmod(b, 2)
            dst = Uc[:, D * f:D * f + D].rearrange("p (g s h) -> p s g h", g=8, h=GH)[:, 4 * half:4 * half + 4]
            return dst, bank[b % 2][0:NC, :].rearrange("p (s g h) -> p s g h", s=4, h=GH)

        with nc.Block() as block:
            @block.sync
            def _(sp):
                for n in range(8):
                    if n >= NR:
                        sp.wait_ge(gl_mm, 2 * (n - NR) + 2)
                    sp.dma_start(ring[:, n % NR, :].rearrange("p (c n) -> p c n", c=KC),
                                 i["w_in"][0].rearrange("(p c) n -> p c n", c=KC)[:, :, 1024 + 256 * n:1280 + 256 * n]
                                 ).then_inc(gate_in[n % NR], 16)
                sp.wait_ge(gl_mm, 16)
                sp.dma_start(w_glu, i["w_glu"][0].rearrange("(k p) n -> p k n", p=P)).then_inc(glu_in, 16)
                sp.dma_start(w_p5, i["w_proj_s5"][0, 0:5 * P, :].rearrange("(k p) n -> p k n", p=P)).then_inc(p5_in, 16)
                sp.wait_ge(fin_row, 2)
                sp.dma_start(o["st_re"][0, 0].rearrange("d (q a) n -> (d q) (a n)", a=2), fin_rows[0]
                             ).then_inc(st_out, 16)
                sp.dma_start(o["st_im"][0, 0].rearrange("d (q a) n -> (d q) (a n)", a=2), fin_rows[1]
                             ).then_inc(st_out, 16)
                sp.wait_ge(st_out, 32)

            @block.tensor
            def _(pe):
                for b in range(NUC):
                    if b >= 2:
                        pe.wait_ge(uc_ok, b - 1)
                    for k in range(4):
                        f, s = divmod(4 * b + k, LC)
                        ins = nc.tensor.transpose(bank[b % 2][0:NC, k * P:(k + 1) * P], uT[:, f, s:TOK:LC], ident)
                    ins.then_inc(uc_T, 1)
                pe.wait_ge(uc_ok, NUC)
                for b in range(6):
                    if b >= 2:
                        pe.wait_ge(u2_ok, b - 1)
                    for k in range(8):
                        ins = nc.tensor.transpose(bank[2 + b % 2][:, k * NC:(k + 1) * NC], Uc[:, P * (8 * b + k):P * (8 * b + k) + P],
                                                  ident[0:NC, 0:NC])
                    ins.then_inc(u2_T, 1)

                def bt(q):
                    if q >= 2:
                        pe.wait_ge(bt_ok, q - 1)
                    for x in range(4):
                        d, r = divmod(x, 2)
                        ins = nc.tensor.transpose(bank[4 + q % 2][:, x * P:(x + 1) * P],
                                                  BP[:, r, d * Q + q].rearrange("p s h -> p (s h)"), ident)
                    ins.then_inc(bt_T, 1)

                def sums(q):
                    pe.wait_ge(bt_ok, q + 1)
                    if q >= 2:
                        pe.wait_ge(v_ok, q - 1)
                    if q == 0:
                        pe.wait_ge(u2_ok, 6)
                    for x in range(4):
                        for a in range(2):
                            ins = nc.tensor.matmul(bank[6 + q % 2][64 * a:64 * a + 64, x * NC:(x + 1) * NC],
                                                   BT[:, q % 4, x, 64 * a:64 * a + 64], U[:, 2 * q + a, :],
                                                   start=True, stop=True)
                    ins.then_inc(v_mm, 1)

                bt(0)
                for q in range(Q):
                    if q + 1 < Q:
                        bt(q + 1)
                    sums(q)
                for m in range(16):
                    n = m // 2
                    pe.wait_ge(gate_in[n % NR], 16 * (n // NR + 1))
                    if m >= 2:
                        pe.wait_ge(gl_ok, m - 1)
                    w = ring[:, n % NR, :].rearrange("p (c n) -> p c n", c=KC)
                    for c in range(KC):
                        ins = nc.tensor.matmul(bank[m % 2][:, 0:TOK], w[:, c, P * (m % 2):P * (m % 2) + P], hT[:, c, :],
                                               start=c == 0, stop=c == KC - 1)
                    ins.then_inc(gl_mm, 1)
                pe.wait_ge(fin_ok, 1)
                for r in range(2):
                    ins = nc.tensor.transpose(bank[2][0:DQ, r * P:(r + 1) * P], fin[:, r], ident)
                ins.then_inc(fin_T, 1)

                def kernels(f):
                    for half in range(2):
                        if f >= 1:
                            pe.wait_ge(t_ok, 2 * (f - 1) + half + 1)
                        for k in range(4):
                            t = 4 * half + k
                            c0 = GH * (LC - 1 - t)
                            ins = nc.tensor.transpose(bank[4 + half][:, k * P:(k + 1) * P], KK[:, f, c0:c0 + P], ident)
                        ins.then_inc(t_T, 1)

                def outputs(f):
                    pe.wait_ge(t_ok, 2 * f + 2)
                    pe.wait_ge(srev_ok, f + 1)
                    if f == 0:
                        pe.wait_ge(scan_ok, 2)
                    if f >= 2:
                        pe.wait_ge(y_ok, f - 1)
                    for q4 in range(4):
                        q = 4 * f + q4
                        out = [bank[6 + f % 2][64 * a:64 * a + NC, P * q4:P * q4 + P] for a in range(2)]
                        for a in range(2):
                            nc.tensor.matmul(out[a], U[:, 2 * q + a, :],
                                             Tt[:, f % 2, 2 * q4 + a].rearrange("p t h -> p (t h)"), start=True, stop=False)
                        for n, (d, r) in enumerate(((0, 0), (0, 1), (1, 0), (1, 1))):
                            for a in range(2):
                                rows_ = slice(64 * a, 64 * a + 64)
                                st = Sin[rows_, r, q, :] if d == 0 else Srev[rows_, f % 2, r, q4, :]
                                ins = nc.tensor.matmul(out[a], st, CP[rows_, r, d * Q + q].rearrange("p t h -> p (t h)"),
                                                       start=False, stop=n == 3)
                    ins.then_inc(y_mm, 1)

                kernels(0)
                for f in range(FT):
                    if f + 1 < FT:
                        kernels(f + 1)
                    outputs(f)

            @block.scalar
            def _(act):
                for b in range(0, NUC, 2):
                    act.wait_ge(uc_T, b + 1)
                    if b:
                        act.wait_ge(uc_ok, b)
                    nc.scalar.activation(*uc_copy(b), ACT.Copy).then_inc(uc_ok, 1)
                for b in range(6):
                    act.wait_ge(u2_T, b + 1)
                    nc.scalar.activation(U[:, 8 * b:8 * b + 8, :].rearrange("p g k -> p (g k)"), bank[2 + b % 2][:, 0:8 * NC],
                                         ACT.Copy).then_inc(u2_ok, 1)
                for q in range(Q):
                    act.wait_ge(bt_T, q + 1)
                    if q >= 4:
                        act.wait_ge(v_mm, q - 3)
                    nc.scalar.activation(BT[:, q % 4].rearrange("p x n -> p (x n)"), bank[4 + q % 2][:, :], ACT.Copy
                                         ).then_inc(bt_ok, 1)
                for m in range(16):
                    act.wait_ge(gl_mm, m + 1)
                    nc.scalar.activation(GLT[:, m, :], bank[m % 2][:, 0:TOK], ACT.Sigmoid).then_inc(gl_ok, 1)
                act.wait_ge(fin_T, 1)
                for r in range(2):
                    nc.scalar.activation(fin_rows[r], bank[2][0:DQ, r * P:(r + 1) * P],
                                         ACT.Copy).then_inc(fin_row, 1)
                act.wait_ge(scan_ok, 2)
                for f in range(FT):
                    if f >= 2:
                        act.wait_ge(y_mm, f - 1)
                    nc.scalar.activation(Srev[:, f % 2], Sin[:, :, Q + 4 * f:Q + 4 * f + 4, ::-1], ACT.Copy).then_inc(srev_ok, 1)
                    act.wait_ge(t_T, 2 * f + 1)
                    if f >= 2:
                        act.wait_ge(y_mm, f - 1)
                    nc.scalar.activation(Tt[:, f % 2, :, 0:4, :].rearrange("p g t h -> p t g h"),
                                         bank[4][:, :].rearrange("p (t g h) -> p t g h", t=4, h=GH), ACT.Copy).then_inc(t_ok, 1)
                    act.wait_ge(t_T, 2 * f + 2)
                    nc.scalar.activation(Tt[:, f % 2, :, 4:8, :].rearrange("p g t h -> p t g h"),
                                         bank[5][:, :].rearrange("p (t g h) -> p t g h", t=4, h=GH), ACT.Copy).then_inc(t_ok, 1)

            @block.vector
            def _(dve):
                scan_c, scan_l = sem("scan_c"), sem("scan_l")
                tt = nc.vector.tensor_tensor
                for b in range(1, NUC, 2):
                    dve.wait_ge(uc_T, b + 1)
                    dve.wait_ge(uc_ok, b)
                    nc.vector.tensor_copy(*uc_copy(b)).then_inc(uc_ok, 1)
                for q in range(Q):
                    dve.wait_ge(v_mm, q + 1)
                    ps = bank[6 + q % 2][:, 0:4 * NC].rearrange("p (d r k) -> p d r k", d=2, r=2)
                    nc.vector.tensor_copy(V[:, :, q, :], ps[:, 0])
                    nc.vector.tensor_copy(V[:, :, Q + q, :], ps[:, 1, :, ::-1]).then_inc(v_ok, 1)
                dve.wait_ge(v_ok, Q)
                S4 = Sin.rearrange("p r (d q) k -> p r d q k", d=2)
                V4 = V.rearrange("p r (d q) k -> p r d q k", d=2)

                def cols(v, ctx_seq, j):
                    f, b = (j, CC * 2 + j) if ctx_seq else (CC + j, j)
                    return v[:, :, 0, :, f], v[:, :, 1, :, b]

                h04 = h0.rearrange("p r (d q) -> p r d q", d=2)
                for d, (c, l) in enumerate(zip(cols(S4, True, 0), cols(S4, False, 0))):
                    nc.vector.memset(c, 0.0)
                    nc.vector.tensor_copy(l, h04[:, :, d]).then_inc(scan_l, 1)
                nc.vector.memset(fin, 0.0).then_inc(scan_c, 1)
                nc.vector.tensor_copy(t3, h0).then_inc(scan_l, 1)
                state = {True: fin, False: t3}
                n_c, n_l = 1, 3
                for j in range(32):
                    for ctx_seq in (True, False):
                        if ctx_seq and j >= CC or not ctx_seq and j == 31:
                            continue
                        s, x, sm = state[ctx_seq], (t1 if ctx_seq else t2), (scan_c if ctx_seq else scan_l)
                        n = n_c if ctx_seq else n_l
                        dve.wait_ge(sm, n)
                        tt(x, Aii, s[:, ::-1, :], ALU.mult).then_inc(sm, 1)
                        dve.wait_ge(sm, n + 1)
                        tt(s, Arr, s, ALU.mult).then_inc(sm, 1)
                        xv = x.rearrange("p r (d q) -> p r d q", d=2)
                        vf, vb = cols(V4, ctx_seq, j)
                        tt(xv[:, :, 0], xv[:, :, 0], vf, ALU.add)
                        tt(xv[:, :, 1], xv[:, :, 1], vb, ALU.add).then_inc(sm, 1)
                        dve.wait_ge(sm, n + 3)
                        last = ctx_seq and j == CC - 1
                        tt(s, s, x, ALU.add).then_inc(fin_ok if last else sm, 1)
                        if not last:
                            dve.wait_ge(sm, n + 4)
                            sv = s.rearrange("p r (d q) -> p r d q", d=2)
                            tf, tb = cols(S4, ctx_seq, j + 1)
                            nc.vector.tensor_copy(tf, sv[:, :, 0])
                            ins = nc.vector.tensor_copy(tb, sv[:, :, 1])
                            if not ctx_seq and j == 30:
                                ins.then_inc(scan_ok, 2)
                        if ctx_seq:
                            n_c += 4
                        else:
                            n_l += 4
                for f in range(FT):
                    dve.wait_ge(y_mm, f + 1)
                    for a in range(2):
                        ins = nc.vector.tensor_copy(
                            Yc[:, :, P * f:P * f + P].rearrange("p t (q a h) -> p t q a h", q=4, a=2)[:, :, :, a, :].rearrange("p t q h -> p q t h"),
                            bank[6 + f % 2][64 * a:64 * a + NC, :].rearrange("p (q t h) -> p q t h", q=4, h=GH))
                    ins.then_inc(y_ok, 1)

        w_p6 = at(o_T, D)
        w_pf = at(o_B, 2 * D).rearrange("p (k n) -> p k n", k=2)
        w_o = at(o_B + 2 * D, KC * D).rearrange("p (k n) -> p k n", k=KC)
        dft = at(o_B + 10 * D, N_DFT)
        gT = at(o_U, FT * TOK).rearrange("p (f t) -> p f t", f=FT)
        AT = at(o_H, FT * TOK).rearrange("p (f t) -> p f t", f=FT)
        yfT = at(o_H + FT * TOK, 2 * TOK).rearrange("p (f t) -> p f t", f=2)
        PQ = at(o_V, 4 * TOK).rearrange("p (f x t) -> p f x t", f=2, x=2)
        sgl = at(o_T + D, 2 * TOK).rearrange("p (b t) -> p b t", b=2)
        pos_t = at(o_V + 2048, 2048).rearrange("p (j n) -> p j n", j=2)
        g2g_b = at(o_V + 4096, D)
        x_new = at(o_V, D).rearrange("p (b n) -> p b n", b=2)
        hs = at(o_V + 5120, 2 * TOK).rearrange("p (f t) -> p f t", f=2)
        X = at(o_W, NT * D).rearrange("p (j n) -> p j n", j=NT)
        H = at(o_W + 3072, NT * D).rearrange("p (j n) -> p j n", j=NT)
        ACC = at(o_W + 6144, NT * D).rearrange("p (j n) -> p j n", j=NT)
        xn = ACC
        g1b, gs2b, sh2b = [at(o_A + 6144 + 2048 * k, 2048).rearrange("p (r n) -> p r n", r=2) for k in range(3)]
        w_r = at(o_ch, KC * E).rearrange("p (c e) -> p c e", c=KC)
        w_s1, w_s3 = [at(b, 2048).rearrange("p (c n) -> p c n", c=KC) for b in (o_B, o_B + 10 * D)]
        w_s2 = at(o_T, 2048).rearrange("p (c n) -> p c n", c=2)
        lgT = at(o_U, TOK, slice(0, E))
        (sc, bi, mx, msk, th8, gtm, eqm, cum, tmpE) = [at(o_U + TOK + 192 * k, 192) for k in range(9)]
        bias_b = at(o_misc + 128, E)
        gsc, rnk, gm, gneg = [misc[:, 192 + 24 * k:216 + 24 * k] for k in range(4)]
        ngt, lim, wsum, wrec = [misc[:, 288 + 4 * k:291 + 4 * k] for k in range(4)]
        posM, GT, cnt, MS = [at(o_K + 2304 + 192 * k, n) for k, n in enumerate((192, 192, 64))] + [at(o_S + 768 - 192, 192)]
        by_tile = lambda v: v.rearrange("p (j e) -> p j e", j=NT)

        (w3_in, dft_in, x2_in, pos2_in, bc_in, wr_in, ws_in, ws2_in) = [sem(n) for n in (
            "w3_in", "dft_in", "x2_in", "pos2_in", "bc_in", "wr_in", "ws_in", "ws2_in")]
        (g_T, g_ok, f1_mm, f1_ok, f2_mm, f2_ok, glu_mm, glu_sg, glu_ok, pr_mm, pr_ok, o_mm, x2_ok) = [sem(n) for n in (
            "g_T", "g_ok", "f1_mm", "f1_ok", "f2_mm", "f2_ok", "glu_mm", "glu_sg", "glu_ok", "pr_mm", "pr_ok", "o_mm", "x2_ok")]
        (n2_sq, n2_ms, n2_rt, n2_xn, n2_T, n2_hT, n2_g, H_ok, r_mm, r_sg, r_T, sel_ok, pos_mm, pos_ok) = [sem(n) for n in (
            "n2_sq", "n2_ms", "n2_rt", "n2_xn", "n2_T", "n2_hT", "n2_g", "H_ok", "r_mm", "r_sg", "r_T", "sel_ok", "pos_mm", "pos_ok")]
        (sh_mm, sh_si, sh_ok, sy_mm, sy_ok, xp_ok) = [sem(n) for n in ("sh_mm", "sh_si", "sh_ok", "sy_mm", "sy_ok", "xp_ok")]

        with nc.Block() as block:
            @block.sync
            def _(sp):
                sp.dma_start(w_p6, i["w_proj_s5"][0, 5 * P:6 * P, :]).then_inc(w3_in, 16)
                sp.dma_start(dft, i["k_dft"]).then_inc(dft_in, 16)
                sp.dma_start(w_pf, i["w_proj_f"][0].rearrange("(k p) n -> p k n", p=P)).then_inc(w3_in, 16)
                sp.dma_start(w_o, i["w_out"][0].rearrange("(k p) n -> p k n", p=P)).then_inc(w3_in, 16)
                for r in range(2):
                    for k, mm in enumerate((2, 4, 3)):
                        sp.dma_start((g1b, gs2b, sh2b)[k][:, r, :], ada_dram[r, mm * D:(mm + 1) * D].partition_broadcast(P)
                                     ).then_inc(bc_in, 16)
                    sp.dma_start(mod[:, r, 3:5, :], ada_dram[r, 3 * D:5 * D].rearrange("(m p c) -> p m c", m=2, c=KC)
                                 ).then_inc(bc_in, 16)
                sp.dma_start(bias_b, i["router_bias"][0].partition_broadcast(P)).then_inc(wr_in, 16)
                sp.dma_start(w_r, i["w_router"][0].rearrange("(p c) e -> p c e", c=KC)).then_inc(wr_in, 16)
                sp.wait_ge(g_ok, 6)
                sp.dma_start(g2g_b, i["norm2_g"][0].partition_broadcast(P)).then_inc(bc_in, 16)
                sp.dma_start(pos_t, i["k_pos"].rearrange("(j p) n -> p j n", p=P)).then_inc(pos2_in, 16)
                sp.wait_ge(glu_mm, 6)
                sp.dma_start(X[:, 0], i["x_prompt"][0]).then_inc(x2_in, 16)
                sp.dma_start(X[:, 1:3], i["x_sample"][0].rearrange("(j p) n -> p j n", p=P)).then_inc(x2_in, 16)
                sp.wait_ge(pr_mm, 8)
                sp.dma_start(w_s1, i["ws1"][0].rearrange("(p c) n -> p c n", c=KC)).then_inc(ws_in, 16)
                sp.dma_start(w_s3, i["ws3"][0].rearrange("(p c) n -> p c n", c=KC)).then_inc(ws_in, 16)
                sp.dma_start(w_s2, i["ws2"][0].rearrange("(p c) n -> p c n", c=2)).then_inc(ws2_in, 16)

            @block.tensor
            def _(pe):
                for f in range(FT):
                    if f >= 2:
                        pe.wait_ge(g_ok, f - 1)
                    for t in range(LC):
                        ins = nc.tensor.transpose(bank[f % 2][:, t * NC:(t + 1) * NC], Yc[:, t, f * P:(f + 1) * P], ident[0:NC, 0:NC])
                    ins.then_inc(g_T, 1)
                pe.wait_ge(dft_in, 16)
                for n in range(4):
                    seq, f = divmod(n, 2)
                    if n >= 2:
                        pe.wait_ge(f1_ok, n - 1)
                    if seq == 0:
                        ins = nc.tensor.matmul(bank[2 + n % 2][:, 0:256], Z[:, 0, f * P:(f + 1) * P], dft[:, F_CTX:F_CTX + 256],
                                               start=True, stop=True)
                    else:
                        for j in range(2):
                            ins = nc.tensor.matmul(bank[2 + n % 2][:, :], Z[:, 1 + j, f * P:(f + 1) * P],
                                                   dft[:, F_LAT + 512 * j:F_LAT + 512 * j + 512], start=j == 0, stop=j == 1)
                    ins.then_inc(f1_mm, 1)
                pe.wait_ge(f1_ok, 4)
                for f in range(2):
                    nc.tensor.matmul(bank[4 + f][:, 0:TOK], dft[:, F_BC:F_BC + P], PQ[:, f, 0, :], start=True, stop=False)
                    nc.tensor.matmul(bank[4 + f][:, 0:TOK], dft[:, F_BS:F_BS + P], PQ[:, f, 1, :], start=False, stop=True
                                     ).then_inc(f2_mm, 1)
                pe.wait_ge(glu_in, 16)
                pe.wait_ge(g_ok, 6)
                for f in range(FT):
                    if f >= 2:
                        pe.wait_ge(glu_sg, f - 1)
                    for k in range(FT):
                        ins = nc.tensor.matmul(bank[6 + f % 2][:, 0:TOK], w_glu[:, k, f * P:(f + 1) * P], gT[:, k, :],
                                               start=k == 0, stop=k == FT - 1)
                    ins.then_inc(glu_mm, 1)
                pe.wait_ge(p5_in, 16)
                pe.wait_ge(w3_in, 48)
                pe.wait_ge(glu_ok, 6)
                pe.wait_ge(f2_ok, 2)
                for m in range(KC):
                    if m >= 2:
                        pe.wait_ge(pr_ok, m - 1)
                    for k in range(FT):
                        w = w_p5[:, k] if k < 5 else w_p6
                        nc.tensor.matmul(bank[m % 2][:, 0:TOK], w[:, m * P:(m + 1) * P], AT[:, k, :], start=k == 0, stop=k == FT - 1)
                    for k in range(2):
                        ins = nc.tensor.matmul(bank[2 + m % 2][:, 0:TOK], w_pf[:, k, m * P:(m + 1) * P], yfT[:, k, :],
                                               start=k == 0, stop=k == 1)
                    ins.then_inc(pr_mm, 1)
                pe.wait_ge(pr_ok, KC)
                for j in range(NT):
                    for n in range(2):
                        if 2 * j + n >= 2:
                            pe.wait_ge(x2_ok, 2 * j + n - 1)
                        for m in range(KC):
                            ins = nc.tensor.matmul(bank[4 + n][:, :], GLT[:, m, j * P:(j + 1) * P], w_o[:, m, 512 * n:512 * n + 512],
                                                   start=m == 0, stop=m == KC - 1)
                        ins.then_inc(o_mm, 1)
                for j in range(NT):
                    pe.wait_ge(n2_xn, j + 1)
                    for h in range(2):
                        if j:
                            pe.wait_ge(n2_hT, 2 * (j - 1) + h + 1)
                        for c in range(4):
                            ins = nc.tensor.transpose(bank[6 + h][:, c * P:(c + 1) * P], xn[:, j, 4 * h + c:D:KC], ident)
                        ins.then_inc(n2_T, 1)
                pe.wait_ge(n2_hT, 6)
                pe.wait_ge(wr_in, 32)
                for c in range(KC):
                    ins = nc.tensor.matmul(bank[0][0:E, 0:TOK], w_r[:, c, :], hT[:, c, :], start=c == 0, stop=c == KC - 1)
                ins.then_inc(r_mm, 1)
                pe.wait_ge(ws_in, 32)
                for f in range(2):
                    for k, w in enumerate((w_s1, w_s3)):
                        for c in range(KC):
                            ins = nc.tensor.matmul(bank[2 + 2 * f + k][:, 0:TOK], w[:, c, f:FE:2], hT[:, c, :],
                                                   start=c == 0, stop=c == KC - 1)
                        ins.then_inc(sh_mm, 1)
                    if f == 0:
                        pe.wait_ge(r_sg, 1)
                        for j in range(NT):
                            ins = nc.tensor.transpose(bank[1][:, j * E:(j + 1) * E], lgT[:, j * P:(j + 1) * P], ident[0:E, 0:E])
                        ins.then_inc(r_T, 1)
                pe.wait_ge(sh_ok, 2)
                pe.wait_ge(ws2_in, 16)
                for j in range(NT):
                    for n in range(2):
                        if 2 * j + n >= 2:
                            pe.wait_ge(sy_ok, 2 * j + n - 1)
                        for f in range(2):
                            ins = nc.tensor.matmul(bank[6 + n][:, :], hs[:, f, j * P:(j + 1) * P], w_s2[:, f, 512 * n:512 * n + 512],
                                                   start=f == 0, stop=f == 1)
                        ins.then_inc(sy_mm, 1)
                pe.wait_ge(sel_ok, 1)
                msv = by_tile(MS)
                for j in range(NT):
                    for k in range(j + 1):
                        nc.tensor.matmul(bank[0][:, j * E:(j + 1) * E], const[:, C_TRI:C_TRI + P] if k == j else const[:, C_ONE:C_ONE + P],
                                         msv[:, k], start=k == 0, stop=k == j)
                for k in range(NT):
                    ins = nc.tensor.matmul(bank[0][:, 3 * E:4 * E], const[:, C_ONE:C_ONE + P], msv[:, k], start=k == 0, stop=k == NT - 1)
                ins.then_inc(pos_mm, 1)

            @block.scalar
            def _(act):
                for f in range(FT):
                    act.wait_ge(g_T, f + 1)
                    nc.scalar.activation(gT[:, f].rearrange("p (k t) -> p t k", t=LC),
                                         bank[f % 2][:, 0:TOK].rearrange("p (t k) -> p t k", t=LC), ACT.Gelu_apprx_tanh
                                         ).then_inc(g_ok, 1)
                for f in range(FT):
                    act.wait_ge(glu_mm, f + 1)
                    if f >= 2:
                        act.wait_ge(glu_ok, f - 1)
                    nc.scalar.activation(sgl[:, f % 2], bank[6 + f % 2][:, 0:TOK], ACT.Sigmoid).then_inc(glu_sg, 1)

                for j in range(NT):
                    act.wait_ge(x2_ok, 2 * j + 2)
                    if j:
                        act.wait_ge(n2_sq, j)
                    nc.scalar.activation(at(o_U, D), X[:, j], ACT.Square,
                                         accum_out=nst[:, j:j + 1]).then_inc(n2_sq, 1)
                    act.wait_ge(n2_ms, j + 1)
                    nc.scalar.activation(nst[:, 8 + j:9 + j], nst[:, 4 + j:5 + j], ACT.Sqrt).then_inc(n2_rt, 1)
                act.wait_ge(n2_g, 1)
                for j in range(NT):
                    r = 0 if j == 0 else 1
                    for h in range(2):
                        act.wait_ge(n2_T, 2 * j + h + 1)
                        for c in range(4):
                            cc = 4 * h + c
                            ins = nc.scalar.activation(hT[:, cc, j * P:(j + 1) * P], bank[6 + h][:, c * P:(c + 1) * P],
                                                       ACT.Identity, scale=gs2[:, r, cc:cc + 1], bias=mod[:, r, 3, cc:cc + 1])
                        ins.then_inc(n2_hT, 1)
                act.wait_ge(r_mm, 1)
                nc.scalar.activation(lgT, bank[0][0:E, 0:TOK], ACT.Sigmoid).then_inc(r_sg, 1)
                for f in range(2):
                    act.wait_ge(sh_mm, 2 * f + 1)
                    nc.scalar.activation(hs[:, f], bank[2 + 2 * f][:, 0:TOK], ACT.Silu).then_inc(sh_si, 1)
                act.wait_ge(H_ok, 3)
                for j in range(NT):
                    for n in range(2):
                        act.wait_ge(sy_mm, 2 * j + n + 1)
                        nc.scalar.activation(ACC[:, j, 512 * n:512 * n + 512], bank[6 + n][:, :], ACT.Copy).then_inc(sy_ok, 1)

            @block.vector
            def _(dve):
                dve_step = sem("dve_step3")
                n_step = [0]

                def step(ins):
                    n_step[0] += 1
                    ins.then_inc(dve_step, 1)
                    dve.wait_ge(dve_step, n_step[0])

                tt, ts, stt = nc.vector.tensor_tensor, nc.vector.tensor_scalar, nc.vector.scalar_tensor_tensor
                dve.wait_ge(g_ok, 6)
                for n in range(4):
                    seq, f = divmod(n, 2)
                    w, t0 = (CTX, 0) if seq == 0 else (LAT, CTX)
                    dve.wait_ge(f1_mm, n + 1)
                    nc.vector.tensor_copy(PQ[:, f, :, t0:t0 + w], bank[2 + n % 2][:, 0:2 * w].rearrange("p (x t) -> p x t", x=2)
                                          ).then_inc(f1_ok, 1)
                for f in range(2):
                    dve.wait_ge(f2_mm, f + 1)
                    nc.vector.tensor_copy(yfT[:, f], bank[4 + f][:, 0:TOK]).then_inc(f2_ok, 1)
                for f in range(FT):
                    dve.wait_ge(glu_sg, f + 1)
                    tt(AT[:, f], gT[:, f], sgl[:, f % 2], ALU.mult).then_inc(glu_ok, 1)
                dve.wait_ge(x2_in, 32)
                dve.wait_ge(pos2_in, 16)
                tt(X[:, 1:3], X[:, 1:3], pos_t, ALU.add).then_inc(xp_ok, 1)
                for m in range(KC):
                    dve.wait_ge(pr_mm, m + 1)
                    tt(GLT[:, m], GLT[:, m], bank[m % 2][:, 0:TOK], ALU.mult)
                    step(tt(GLT[:, 8 + m], GLT[:, 8 + m], bank[2 + m % 2][:, 0:TOK], ALU.mult))
                    tt(GLT[:, m], GLT[:, m], GLT[:, 8 + m], ALU.add).then_inc(pr_ok, 1)
                dve.wait_ge(bc_in, 144)
                for r in range(2):
                    stt(out=gs2[:, r], in0=mod[:, r, 4, :], scalar=1.0, in1=g2n, op0=ALU.add, op1=ALU.mult)
                    ins = stt(out=gs2b[:, r], in0=gs2b[:, r], scalar=1.0, in1=g2g_b, op0=ALU.add, op1=ALU.mult)
                ins.then_inc(n2_g, 1)
                dve.wait_ge(xp_ok, 1)
                for j in range(NT):
                    r = 0 if j == 0 else 1
                    for n in range(2):
                        cols_ = slice(512 * n, 512 * n + 512)
                        dve.wait_ge(o_mm, 2 * j + n + 1)
                        step(tt(x_new[:, n], bank[4 + n][:, :], g1b[:, r, cols_], ALU.mult))
                        tt(X[:, j, cols_], X[:, j, cols_], x_new[:, n], ALU.add).then_inc(x2_ok, 1)
                for j in range(NT):
                    r = 0 if j == 0 else 1
                    dve.wait_ge(n2_sq, j + 1)
                    ts(nst[:, 4 + j:5 + j], nst[:, j:j + 1], 1.0 / D, EPS, ALU.mult, ALU.add).then_inc(n2_ms, 1)
                    dve.wait_ge(n2_rt, j + 1)
                    step(nc.vector.reciprocal(nst[:, 12 + j:13 + j], nst[:, 8 + j:9 + j]))
                    ts(xn[:, j], X[:, j], nst[:, 12 + j:13 + j], None, ALU.mult).then_inc(n2_xn, 1)
                dve.wait_ge(n2_T, 6)
                dve.wait_ge(n2_g, 1)
                dve.wait_ge(n2_xn, 3)
                for j in range(NT):
                    r = 0 if j == 0 else 1
                    step(tt(xn[:, j], xn[:, j], gs2b[:, r], ALU.mult))
                    tt(H[:, j].rearrange("p (c q) -> p q c", c=KC), xn[:, j].rearrange("p (q c) -> p q c", c=KC),
                       sh2b[:, r].rearrange("p (q c) -> p q c", c=KC), ALU.add).then_inc(H_ok, 1)
                for f in range(2):
                    dve.wait_ge(sh_mm, 2 * f + 2)
                    dve.wait_ge(sh_si, f + 1)
                    tt(hs[:, f], hs[:, f], bank[3 + 2 * f][:, 0:TOK], ALU.mult).then_inc(sh_ok, 1)
                dve.wait_ge(r_T, 1)
                step(nc.vector.tensor_copy(sc, bank[1][:, 0:NT * E]))
                step(tt(by_tile(bi), by_tile(sc), bias_b.unsqueeze(1).to_broadcast([P, NT, E]), ALU.add))
                for g in range(NT * EG):
                    ins = nc.vector.max(mx[:, 8 * g:8 * g + 8], bi[:, EGS * g:EGS * g + EGS])
                step(ins)
                mxv = mx.rearrange("p (g k) -> p g k", k=8)
                step(tt(gsc, mxv[:, :, 0], mxv[:, :, 1], ALU.add))
                gi = gsc.rearrange("p (j g) -> p j g", j=NT).unsqueeze(3).to_broadcast([P, NT, EG, EG])
                gj = gsc.rearrange("p (j g) -> p j g", j=NT).unsqueeze(2).to_broadcast([P, NT, EG, EG])
                r4 = lambda v: v.rearrange("p (j a b) -> p j a b", j=NT, a=EG)
                low = const[:, C_LOW:C_LOW + 64].rearrange("p (a b) -> p a b", a=EG).unsqueeze(1).to_broadcast([P, NT, EG, EG])
                tt(r4(gtm), gj, gi, ALU.is_gt)
                step(tt(r4(eqm), gj, gi, ALU.is_equal))
                step(tt(r4(eqm), r4(eqm), low, ALU.mult))
                step(tt(gtm, gtm, eqm, ALU.add))
                step(nc.vector.tensor_reduce(rnk, gtm.rearrange("p (g k) -> p g k", k=EG), AX_X, ALU.add))
                step(ts(gm, rnk, float(EGK), None, ALU.is_lt))
                step(ts(gneg, gm, BIG, -BIG, ALU.mult, ALU.add))
                g8 = lambda v: v.rearrange("p (g k) -> p g k", k=EGS)
                step(tt(g8(msk), g8(bi), gm.unsqueeze(2).to_broadcast([P, NT * EG, EGS]), ALU.mult))
                step(tt(g8(msk), g8(msk), gneg.unsqueeze(2).to_broadcast([P, NT * EG, EGS]), ALU.add))
                for j in range(NT):
                    ins = nc.vector.max(th8[:, 8 * j:8 * j + 8], msk[:, E * j:E * j + E])
                step(ins)
                for j in range(NT):
                    th = th8[:, 8 * j + TOPK - 1:8 * j + TOPK]
                    ts(gtm[:, E * j:E * j + E], msk[:, E * j:E * j + E], th, None, ALU.is_gt)
                    ins = ts(eqm[:, E * j:E * j + E], msk[:, E * j:E * j + E], th, None, ALU.is_equal)
                step(ins)
                step(nc.vector.tensor_reduce(ngt, by_tile(gtm), AX_X, ALU.add))
                ts(lim, ngt, -1.0, float(TOPK), ALU.mult, ALU.add)
                for j in range(NT):
                    ins = nc.vector.tensor_tensor_scan(cum[:, E * j:E * j + E], eqm[:, E * j:E * j + E], eqm[:, E * j:E * j + E],
                                                       0.0, ALU.add, ALU.bypass)
                step(ins)
                for j in range(NT):
                    ins = stt(out=cum[:, E * j:E * j + E], in0=cum[:, E * j:E * j + E], scalar=lim[:, j:j + 1],
                              in1=eqm[:, E * j:E * j + E], op0=ALU.is_le, op1=ALU.mult)
                step(ins)
                tt(MS, gtm, cum, ALU.add).then_inc(sel_ok, 1)
                dve.wait_ge(sel_ok, 1)
                step(tt(tmpE, sc, MS, ALU.mult))
                step(nc.vector.tensor_reduce(wsum, by_tile(tmpE), AX_X, ALU.add))
                step(nc.vector.reciprocal(wrec, wsum))
                for j in range(NT):
                    ts(GT[:, E * j:E * j + E], tmpE[:, E * j:E * j + E], wrec[:, j:j + 1], SCALE, ALU.mult, ALU.mult)
                dve.wait_ge(pos_mm, 1)
                step(stt(out=posM, in0=bank[0][:, 0:NT * E], scalar=1.0, in1=MS, op0=ALU.add, op1=ALU.mult))
                ts(posM, posM, 1.0, None, ALU.subtract)
                nc.vector.tensor_copy(cnt, bank[0][:, 3 * E:4 * E]).then_inc(pos_ok, 1)

        SLOTS = BATCH * SL
        MAXT = 40
        assert MAXT >= TOK * TOPK // (SL + 1) and MAXT % BATCH == 0 and MAXT <= E
        slot = [at(o_A + 6144 * k, 6144) for k in range(RING)]
        slot13 = [v[:, 0:4096].rearrange("p (w c n) -> p w c n", w=2, c=KC) for v in slot]
        slot2 = [v[:, 4096:6144].rearrange("p (f n) -> p f n", f=2) for v in slot]
        g2b = at(o_T, 2 * D).rearrange("p (r n) -> p r n", r=2)
        fin_g = at(o_W + 9216, D)
        XT = at(o_V, KC * SLOTS).rearrange("p (c s) -> p c s", c=KC)
        S = at(o_V + 4096, NT * SLOTS).rearrange("p (j s) -> p j s", j=NT)
        OH = at(o_V + 5632, 512)
        Y = at(o_H, 4 * D).rearrange("p (q n) -> p q n", q=4)
        hid = at(o_H + 4096, 512).rearrange("p (b f) -> p b f", b=2)
        hidT = at(o_H + 4608, 256).rearrange("p (f s) -> p f s", f=2)
        silu = at(o_H + 4864, FE)
        ST = at(o_K, 4 * TOK).rearrange("p (q t) -> p q t", q=4)
        Sg = at(o_K + 1536, 2 * TOK).rearrange("p (b j s) -> p b j s", b=2, j=NT)
        tmp512 = at(o_ch, 512)
        pm8, ga8 = misc[:, 384:408], misc[:, 408:432]
        n_ex, cum_ex, pfx = [at(o_const + C_TRI + E * k, E) for k in range(3)]
        posr = at(o_const + C_ONE + E, E)
        ids, idx_f = misc[0:1, 432:432 + MAXT + 1].bitcast(I32), misc[0:1, 480:480 + MAXT]
        k64, five = misc[:, 520:528], misc[0:1, 472:477]
        iota = const[:, C_IOTA:C_IOTA + E]
        gate_flat = at(o_K + 2496, 256)
        pos_flat = at(o_K + 2304, 256)

        w_in = [sem(f"expert_in{k}") for k in range(RING)]
        (fin_in, S_ok, g_mm, xa, xd, h_mm, silu_ok, hid_ok, hidT_mm, hidT_ok, y0_mm, w_used, ya, yd, sg_ok, st_mm, st_ok,
         sc_mm, acc_ok, pm_ok, tail_ok, tail_step, fin_step, x3_ok, fin_sq, fin_ms, fin_rt, y_ready, y_out) = [sem(n) for n in (
             "fin_in", "S_ok", "gather_mm", "xt_act", "xt_dve", "h_mm", "silu_ok", "hid_ok", "hidT_mm", "hidT_ok", "y0_mm",
             "w_used", "y_act", "y_dve", "sg_ok", "st_mm", "st_ok", "scatter_mm", "acc_ok", "pm_ok", "tail_ok", "tail_step",
             "fin_step", "x3_ok", "fin_sq", "fin_ms", "fin_rt", "y_ready", "y_out")]
        NB = E // BATCH

        def wait_last(eng, s, value):
            if not isinstance(value, int) or value > 0:
                eng.wait_ge(s, value)

        def batches(eng, body):
            body(lambda per, off=0: off, BATCH)
            with eng.Fori(0, NB - 1) as b:
                body(lambda per, off=0: b * per + (per + off), b * BATCH + 2 * BATCH)
            eng.wait_ge(tail_ok, 1)
            more = eng.value_load(ids[0:1, 0:1], min_val=0, max_val=MAXT // BATCH)
            with eng.If(more > 0):
                with eng.Fori(0, more) as b:
                    body(lambda per, off=0: b * per + (NB * per + off), None)
            return more

        with nc.Block() as block:
            @block.sync
            def _(sp):
                w1 = i["w1"][0].rearrange("e (p c) n -> p e (c n)", c=KC)
                w3 = i["w3"][0].rearrange("e (p c) n -> p e (c n)", c=KC)
                w2 = i["w2"][0].rearrange("e (p c) n -> p e (c n)", c=2)

                def load(k, e):
                    for n, w in enumerate((w1, w3, w2)):
                        sp.dma_start(slot[k][:, 2048 * n:2048 * n + 2048], w[:, e, :]).then_inc(w_in[k], 16)

                for k in range(RING):
                    load(k, slice(k, k + 1))
                    if k == 0:
                        for r in range(2):
                            sp.dma_start(g2b[:, r, :], ada_dram[r, 5 * D:6 * D].partition_broadcast(P)).then_inc(fin_in, 16)
                        sp.dma_start(fin_g, i["final_norm_g"].partition_broadcast(P)).then_inc(fin_in, 16)
                with sp.Fori(0, E // RING - 1) as g:
                    for k in range(RING):
                        sp.wait_ge(w_used, g * RING + (k + 1))
                        load(k, bass.ds(g * RING + (RING + k), 1))
                sp.wait_ge(tail_ok, 1)
                more = sp.value_load(ids[0:1, 0:1], min_val=0, max_val=MAXT // BATCH)
                with sp.If(more > 0):
                    with sp.Fori(0, more) as b:
                        for k in range(BATCH):
                            e = sp.value_load(ids[0:1, bass.ds(b * BATCH + (k + 1), 1)], min_val=0, max_val=E - 1)
                            sp.wait_ge(w_used, b * BATCH + (E + k - RING + 1))
                            load(k % RING, bass.ds(e, 1))
                sp.wait_ge(y_ready, 1)
                sp.dma_start(o["y_prompt"][0], H[:, 0]).then_inc(y_out, 16)
                sp.wait_ge(y_ready, 3)
                sp.dma_start(o["y_sample"][0].rearrange("(j p) n -> p j n", p=P), H[:, 1:3]).then_inc(y_out, 16)
                sp.wait_ge(y_out, 32)

            @block.tensor
            def _(pe):
                def body(n, following):
                    def hidden(p):
                        if p == 0:
                            pe.wait_ge(xa, n(4, 4))
                            pe.wait_ge(xd, n(4, 4))
                        for a in range(2):
                            pe.wait_ge(w_in[(2 * p + a) % RING], n(96, 48 * ((2 * p + a) // RING + 1)))
                        wait_last(pe, hid_ok, n(4, p - 1 if p >= 2 else 0))
                        for c in range(KC):
                            for a in range(2):
                                ins = nc.tensor.matmul(bank[2 + p % 2][64 * a:64 * a + 64, :],
                                                       XT[:, c, SL * (2 * p + a):SL * (2 * p + a + 1)],
                                                       slot13[(2 * p + a) % RING][:, :, c, :], start=c == 0, stop=c == KC - 1)
                        ins.then_inc(h_mm, 1)
                        pe.wait_ge(sg_ok, n(4, p + 1))
                        wait_last(pe, st_ok, n(4, p))
                        for j in range(NT):
                            ins = nc.tensor.transpose(bank[7][:, j * P:(j + 1) * P], Sg[:, p % 2, j, :], ident)
                        ins.then_inc(st_mm, 1)

                    def down(p):
                        pe.wait_ge(hid_ok, n(4, p + 1))
                        for f in range(2):
                            ins = nc.tensor.transpose(bank[4][:, f * P:(f + 1) * P], hid[:, p % 2, f:FE:2], ident)
                        ins.then_inc(hidT_mm, 1)
                        pe.wait_ge(hidT_ok, n(4, p + 1))
                        wait_last(pe, ya, n(4, p))
                        wait_last(pe, yd, n(4, p))
                        for h in range(2):
                            for f in range(2):
                                for a in range(2):
                                    ins = nc.tensor.matmul(bank[5 + h][64 * a:64 * a + 64, :], hidT[:, f, 64 * a:64 * a + 64],
                                                           slot2[(2 * p + a) % RING][:, f, 512 * h:512 * h + 512],
                                                           start=f == 0, stop=f == 1)
                            ins.then_inc(*((y0_mm, 1) if h == 0 else (w_used, 2)))

                    pe.wait_ge(S_ok, n(1, 1 if following is not None else 2))
                    for c in range(KC):
                        if c < 2:
                            wait_last(pe, acc_ok, n(6))
                        else:
                            pe.wait_ge((xa, xd)[c % 2], n(4, c // 2))
                        for j in range(NT):
                            ins = nc.tensor.matmul(bank[c % 2][:, :], H[:, j, c * P:(c + 1) * P], S[:, j, :],
                                                   start=j == 0, stop=j == NT - 1)
                        ins.then_inc(g_mm, 1)
                    hidden(0)
                    hidden(1)
                    down(0)
                    hidden(2)
                    down(1)
                    hidden(3)
                    down(2)
                    down(3)
                    pe.wait_ge(st_ok, n(4, 4))
                    pe.wait_ge(ya, n(4, 4))
                    pe.wait_ge(yd, n(4, 4))
                    for m in range(2 * NT):
                        j, h = divmod(m, 2)
                        if m >= 2:
                            pe.wait_ge(acc_ok, n(6, m - 1))
                        for p in range(4):
                            ins = nc.tensor.matmul(bank[m % 2][:, :], ST[:, p, j * P:(j + 1) * P], Y[:, p, 512 * h:512 * h + 512],
                                                   start=p == 0, stop=p == 3)
                        ins.then_inc(sc_mm, 1)

                batches(pe, body)

            @block.scalar
            def _(act):
                def body(n, following):
                    def first(p):
                        act.wait_ge(h_mm, n(4, p + 1))
                        wait_last(act, hid_ok, n(4, p))
                        nc.scalar.activation(silu, bank[2 + p % 2][:, 0:FE], ACT.Silu).then_inc(silu_ok, 1)
                        act.wait_ge(st_mm, n(4, p + 1))
                        nc.scalar.activation(ST[:, p], bank[7][:, 0:TOK], ACT.Copy).then_inc(st_ok, 1)

                    def second(p):
                        act.wait_ge(hidT_mm, n(4, p + 1))
                        nc.scalar.activation(hidT.rearrange("p f s -> p (f s)"), bank[4][:, 0:2 * P], ACT.Copy).then_inc(hidT_ok, 1)
                        act.wait_ge(y0_mm, n(4, p + 1))
                        nc.scalar.activation(Y[:, p, 0:512], bank[5][:, :], ACT.Copy).then_inc(ya, 1)

                    for c in range(0, KC, 2):
                        act.wait_ge(g_mm, n(8, c + 1))
                        nc.scalar.activation(XT[:, c], bank[0][:, :], ACT.Copy).then_inc(xa, 1)
                    wait_last(act, sc_mm, n(6))
                    first(0)
                    first(1)
                    second(0)
                    first(2)
                    second(1)
                    first(3)
                    second(2)
                    second(3)

                more = batches(act, body)
                act.wait_ge(fin_in, 48)
                for j in range(NT):
                    act.wait_ge(x3_ok, j + 1)
                    nc.scalar.activation(XT.rearrange("p c s -> p (c s)")[:, j * D:(j + 1) * D], X[:, j], ACT.Square,
                                         accum_out=nst[:, j:j + 1]).then_inc(fin_sq, 1)
                    act.wait_ge(fin_ms, j + 1)
                    nc.scalar.activation(nst[:, 8 + j:9 + j], nst[:, 4 + j:5 + j], ACT.Sqrt).then_inc(fin_rt, 1)

            @block.vector
            def _(dve):
                tt, ts, stt = nc.vector.tensor_tensor, nc.vector.tensor_scalar, nc.vector.scalar_tensor_tensor
                v8 = lambda v: v.rearrange("p (k s) -> p k s", k=BATCH)
                iota8 = iota.unsqueeze(1).to_broadcast([P, BATCH, SL])

                def slots():
                    for j in range(NT):
                        ins = tt(v8(S[:, j]), iota8, pm8[:, 8 * j:8 * j + 8].unsqueeze(2).to_broadcast([P, BATCH, SL]),
                                 ALU.is_equal)
                    ins.then_inc(S_ok, 1)

                def pick(cols_):
                    for j in range(NT):
                        nc.vector.tensor_copy(pm8[:, 8 * j:8 * j + 8], pos_flat[:, cols_(j)])
                    for j in range(NT):
                        ins = nc.vector.tensor_copy(ga8[:, 8 * j:8 * j + 8], gate_flat[:, cols_(j)])
                    ins.then_inc(pm_ok, 1)

                def body(n, following):
                    if following is None:
                        tail_slots(n)
                    for c in range(1, KC, 2):
                        dve.wait_ge(g_mm, n(8, c + 1))
                        nc.vector.tensor_copy(XT[:, c], bank[1][:, :]).then_inc(xd, 1)

                    def gated(p):
                        if p >= 2:
                            dve.wait_ge(st_mm, n(4, p - 1))
                        elif p == 0:
                            wait_last(dve, st_mm, n(4))
                            dve.wait_ge(S_ok, n(1, 1 if following is not None else 2))
                        for j in range(NT):
                            g = ga8[:, 8 * j + 2 * p:8 * j + 2 * p + 2].unsqueeze(2).to_broadcast([P, 2, SL])
                            ins = tt(Sg[:, p % 2, j].rearrange("p (a s) -> p a s", a=2),
                                     S[:, j, 2 * SL * p:2 * SL * (p + 1)].rearrange("p (a s) -> p a s", a=2), g, ALU.mult)
                        ins.then_inc(sg_ok, 1)

                    def hidden(p):
                        dve.wait_ge(silu_ok, n(4, p + 1))
                        tt(hid[:, p % 2], silu, bank[2 + p % 2][:, FE:2 * FE], ALU.mult).then_inc(hid_ok, 1)

                    def down(p):
                        dve.wait_ge(w_used, n(8, 2 * p + 2))
                        if p == 0:
                            wait_last(dve, sc_mm, n(6))
                        nc.vector.tensor_copy(Y[:, p, 512:1024], bank[6][:, :]).then_inc(yd, 1)

                    gated(0)
                    gated(1)
                    hidden(0)
                    gated(2)
                    hidden(1)
                    down(0)
                    gated(3)
                    if following is not None:
                        dve.wait_ge(sg_ok, n(4, 4))
                        pick(lambda j: bass.ds(following + j * E, BATCH))
                        dve.wait_ge(pm_ok, n(1, 2))
                        slots()
                    hidden(2)
                    down(1)
                    hidden(3)
                    down(2)
                    down(3)
                    for m in range(2 * NT):
                        j, h = divmod(m, 2)
                        dve.wait_ge(sc_mm, n(6, m + 1))
                        wait_last(dve, acc_ok, n(6, m))
                        tt(ACC[:, j, 512 * h:512 * h + 512], ACC[:, j, 512 * h:512 * h + 512], bank[m % 2][:, :], ALU.add
                           ).then_inc(acc_ok, 1)

                TS = 18

                def tail_slots(n):
                    count = [0]

                    def step(ins):
                        count[0] += 1
                        ins.then_inc(tail_step, 1)
                        dve.wait_ge(tail_step, n(TS, count[0] - NB * TS))

                    kb = iota[:, 0:BATCH].unsqueeze(2).to_broadcast([P, BATCH, E])
                    row = lambda v: v.unsqueeze(1).to_broadcast([P, BATCH, E])
                    oh, t8 = OH.rearrange("p (k e) -> p k e", k=BATCH), tmp512.rearrange("p (k e) -> p k e", k=BATCH)
                    tt(oh, kb, row(pfx), ALU.is_ge)
                    step(tt(t8, kb, row(cum_ex), ALU.is_lt))
                    step(tt(oh, oh, t8, ALU.mult))
                    for j in range(NT):
                        step(stt(out=posr, in0=pfx, scalar=float(SL), in1=pos_flat[:, j * E:j * E + E], op0=ALU.mult, op1=ALU.add))
                        step(tt(t8, oh, row(posr), ALU.mult))
                        step(nc.vector.tensor_reduce(pm8[:, 8 * j:8 * j + 8], t8, AX_X, ALU.add))
                        step(tt(t8, oh, row(GT[:, j * E:j * E + E]), ALU.mult))
                        step(nc.vector.tensor_reduce(ga8[:, 8 * j:8 * j + 8], t8, AX_X, ALU.add))
                    ts(pfx, pfx, float(BATCH), None, ALU.subtract)
                    step(ts(cum_ex, cum_ex, float(BATCH), None, ALU.subtract))
                    assert count[0] == TS, count[0]
                    for j in range(NT):
                        ins = tt(pm8[:, 8 * j:8 * j + 8], pm8[:, 8 * j:8 * j + 8], k64, ALU.subtract)
                    ins.then_inc(pm_ok, 1)
                    dve.wait_ge(pm_ok, n(1, 2))
                    dve.wait_ge(g_mm, n(8))
                    slots()

                pick(lambda j: slice(j * E, j * E + BATCH))
                dve.wait_ge(pm_ok, 1)
                slots()
                steps = [0]

                def step(ins):
                    steps[0] += 1
                    ins.then_inc(fin_step, 1)
                    dve.wait_ge(fin_step, steps[0])

                step(ts(n_ex, cnt, float(SL), None, ALU.is_gt))
                for r in range(2, TOK // SL):
                    step(stt(out=n_ex, in0=cnt, scalar=float(SL * r), in1=n_ex, op0=ALU.is_gt, op1=ALU.add))
                step(nc.vector.tensor_tensor_scan(cum_ex, n_ex, n_ex, 0.0, ALU.add, ALU.bypass))
                ts(k64, iota[:, 0:BATCH], float(SL), float(SL), ALU.mult, ALU.add)
                step(tt(pfx, cum_ex, n_ex, ALU.subtract))
                who, lim_ = [at(o_H + MAXT * E * k, MAXT * E, slice(0, 1)).rearrange("p (k e) -> p k e", k=MAXT) for k in range(2)]
                item = iota[0:1, 0:MAXT].unsqueeze(2).to_broadcast([1, MAXT, E])
                row1 = lambda v: v[0:1].unsqueeze(1).to_broadcast([1, MAXT, E])
                tt(who, item, row1(pfx), ALU.is_ge)
                step(tt(lim_, item, row1(cum_ex), ALU.is_lt))
                step(tt(who, who, lim_, ALU.mult))
                step(tt(who, who, row1(iota), ALU.mult))
                nc.vector.tensor_reduce(idx_f, who, AX_X, ALU.add)
                step(ts(five, iota[0:1, 0:5], float(BATCH), cum_ex[0:1, E - 1:E], ALU.mult, ALU.is_lt))
                step(nc.vector.tensor_reduce(misc[0:1, 478:479], five, AX_X, ALU.add))
                nc.vector.tensor_copy(ids[:, 1:1 + MAXT], idx_f)
                nc.vector.tensor_copy(ids[:, 0:1], misc[0:1, 478:479]).then_inc(tail_ok, 1)

                more = batches(dve, body)
                dve.wait_ge(acc_ok, more * 6 + 6 * NB)
                dve.wait_ge(fin_in, 48)
                for j in range(NT):
                    r = 0 if j == 0 else 1
                    step(tt(ACC[:, j], ACC[:, j], g2b[:, r], ALU.mult))
                    tt(X[:, j], X[:, j], ACC[:, j], ALU.add).then_inc(x3_ok, 1)
                dve.wait_ge(x3_ok, 3)
                for j in range(NT):
                    dve.wait_ge(fin_sq, j + 1)
                    ts(nst[:, 4 + j:5 + j], nst[:, j:j + 1], 1.0 / D, EPS, ALU.mult, ALU.add).then_inc(fin_ms, 1)
                    dve.wait_ge(fin_rt, j + 1)
                    step(nc.vector.reciprocal(nst[:, 12 + j:13 + j], nst[:, 8 + j:9 + j]))
                    stt(out=H[:, j], in0=X[:, j], scalar=nst[:, 12 + j:13 + j], in1=fin_g, op0=ALU.mult, op1=ALU.mult
                        ).then_inc(y_ready, 1)


_INS = ("x_prompt", "x_sample", "state_s5_re", "state_s5_im", "c", "c_ctx", "w_ada", "b_ada", "norm1_g", "norm2_g",
        "w_in", "lam_re", "lam_im", "log_dt", "b_re", "b_im", "c_re", "c_im", "d_skip", "w_glu", "w_proj_s5", "w_proj_f",
        "w_out", "w_router", "router_bias", "w1", "w3", "w2", "ws1", "ws3", "ws2", "final_norm_g")


def kernel(**inputs):
    import concourse.bacc as bacc
    from concourse.bass_utils import run_bass_kernel_spmd

    nc = bacc.Bacc("TRN2", target_bir_lowering=False, num_devices=1)
    arrays = {name: np.ascontiguousarray(inputs[name]) for name in _INS}
    arrays.update(zip(("k_const", "k_dft", "k_pos"), shape_constants()))
    i = {name: nc.dram_tensor(name, a.shape, mybir.dt.from_np(a.dtype), kind="ExternalInput").ap() for name, a in arrays.items()}
    o = {name: nc.dram_tensor(name, shape, F32, kind="ExternalOutput").ap() for name, shape in OUTS.items()}
    build(nc, i, o)
    r = run_bass_kernel_spmd(nc, [arrays], core_ids=[0])
    return tuple(r.results[0][name] for name in OUTS)
```

```python
from contextlib import ExitStack

import numpy as np

import concourse.bass as bass
from concourse import mybir

F32 = mybir.dt.float32
F32R = mybir.dt.float32r
I32 = mybir.dt.int32
ALU = mybir.AluOpType
ACT = mybir.ActivationFunctionType
AX_X = mybir.AxisListType.X

P = 128
D = 1024
CTX, LAT = 128, 256
TOK = CTX + LAT
NT = TOK // P
GRID_W = 64
KC = D // P
DS = 768
FT = DS // P
DF = 256
G, GH, NS = 48, 16, 64
Q = G // 2
DQ = 2 * Q
LC = 8
NC = TOK // LC
CC = CTX // LC
KW = (2 * LC - 1) * GH
E, TOPK, EG, EGS, EGK = 64, 6, 8, 8, 4
FE = 256
SL = 64
BATCH = 8
RING = 4
EPS = 1e-6
SCALE = 2.5
MAGIC = 1.5 * 2.0 ** 23
PI_A, PI_B, PI_C = 6.28125, 0.0019350051879882812, 3.0199157663701e-07
BIG = 1e30

C_ID, C_TRI, C_ONE, C_IOTA, C_M16, C_PAR, C_LOW = 0, 128, 256, 384, 448, 464, 496
N_CONST = 560
F_CTX, F_LAT, F_BC, F_BS = 0, 256, 1280, 1408
N_DFT = 1536


OUTS = dict(y_prompt=(1, CTX, D), y_sample=(1, LAT, D), st_re=(1, 1, 2, G, NS), st_im=(1, 1, 2, G, NS))


def shape_constants():
    p = np.arange(P)
    k = np.zeros((P, N_CONST), np.float32)
    k[:, C_ID:C_ID + P] = np.eye(P)
    k[:, C_TRI:C_TRI + P] = p[:, None] < p[None, :]
    k[:, C_ONE:C_ONE + P] = 1.0
    k[:, C_IOTA:C_IOTA + 64] = np.arange(64)
    k[:, C_M16:C_M16 + GH] = (p[:, None] % GH) == np.arange(GH)
    k[:, C_PAR:C_PAR + 32] = (p[:, None] // NS) == (np.arange(32) // GH)
    k[:, C_LOW:C_LOW + 64] = (np.arange(8)[:, None] > np.arange(8)[None, :]).reshape(-1)
    f = np.zeros((P, N_DFT))

    def dft(n):
        a = 2 * np.pi * (np.outer(np.arange(n), np.arange(n)) % n) / n
        return np.cos(a) / np.sqrt(n), np.sin(a) / np.sqrt(n)

    c, s = dft(CTX)
    f[:, F_CTX:F_CTX + 256] = np.concatenate([c, s], 1)
    c, s = dft(LAT)
    f[:, F_LAT:F_LAT + 1024] = np.concatenate([c, s], 1).reshape(2, P, 512).transpose(1, 0, 2).reshape(P, 1024)
    c, s = dft(64)
    f[:, F_BC:F_BC + P] = np.kron(np.eye(2), c)
    f[:, F_BS:F_BS + P] = -np.kron(np.eye(2), s)
    quarter = D // 4
    omega = (1.0 / (10000.0 ** (np.arange(quarter, dtype=np.float32) / quarter))).astype(np.float32)

    def emb(pos):
        a = pos.astype(np.float32)[:, None] * omega
        return np.concatenate([np.sin(a), np.cos(a)], -1)

    t = np.arange(LAT)
    pos = np.concatenate([emb(t // GRID_W), emb(t % GRID_W)], -1).astype(np.float32)
    return k, f.astype(np.float32), pos


def build(nc, i, o):
    with ExitStack() as ctx:
        def sem(name):
            return ctx.enter_context(nc.semaphore(name))

        bank = [ctx.enter_context(nc.psum_tensor(f"bank{n}", [P, 512], F32)) for n in range(8)]

        top = [0]

        def region(n):
            top[0] += n
            return top[0] - n


        o_const, o_mod, o_misc = region(N_CONST), region(96), region(528)
        o_A, o_B = region(12288), region(12288)
        o_V, o_K, o_S, o_Z, o_ch = region(6144), region(1440), region(768), region(768), region(576)
        o_W, o_H, o_U, o_T = region(10240), region(3072), region(2304), region(2048)

        sb = ctx.enter_context(nc.sbuf_tensor("sb", [P, o_W], F32))
        first_stages = ctx.enter_context(ExitStack())
        early = first_stages.enter_context(nc.sbuf_tensor("early", [P, top[0] - o_W], F32))

        def at(base, n, rows=slice(0, P)):
            return sb[rows, base:base + n] if base < o_W else early[rows, base - o_W:base - o_W + n]

        const = at(o_const, N_CONST)
        ident = const[:, C_ID:C_ID + P]
        mod = at(o_mod, 96).rearrange("p (r m c) -> p r m c", r=2, m=6)
        misc = at(o_misc, 528)
        ada_dram = nc.dram_tensor("ada_dram", [2, 6 * D], F32).ap()
        x2_dram = nc.dram_tensor("x2_dram", [P, NT, D], F32).ap()


        chan = at(o_ch, 576).rearrange("p (a n) -> p a n", n=DQ)
        a_pow = [chan[:, 2 * k:2 * k + 2, :] for k in range(3)]
        Arr, Aii = chan[:, 6:8, :], chan[:, 8:10, :]
        h0 = chan[:, 10:12, :]

        BP = at(o_A, 12288).rearrange("p (r n s h) -> p r n s h", r=2, n=DQ, h=GH)
        CP = at(o_B, 12288).rearrange("p (r n s h) -> p r n s h", r=2, n=DQ, h=GH)
        KK = at(o_K, FT * KW).rearrange("p (f k) -> p f k", f=FT)
        hT = at(o_H, KC * TOK).rearrange("p (c t) -> p c t", c=KC)
        uT = at(o_U, FT * TOK).rearrange("p (f t) -> p f t", f=FT)
        Z = at(o_Z, 768).rearrange("p (j n) -> p j n", j=NT)

        dve_step, n_step = sem("dve_step"), [0]

        NR = 5
        ring = at(o_W, NR * 2048).rearrange("p (s n) -> p s n", s=NR)
        items = [("ada", 0, c) for c in range(KC + 1)] + [("in", 0, c) for c in range(4)]
        items += [("ada", b, c) for b in (1, 2) for c in range(KC + 1)]
        where = {it: n for n, it in enumerate(items)}
        ring_in = [sem(f"ring_in{n}") for n in range(NR)]
        ring_used = sem("ring_used")
        s_const, s_cond, s_rows, s_c, s_b, s_dg = [sem(n) for n in ("s_const", "s_cond", "s_rows", "s_c", "s_b", "s_dg")]
        s_x = [sem(f"s_x{n}") for n in range(3)]
        s_pos = [sem(f"s_pos{n}") for n in range(2)]
        s_csil, ada_row, ada_out, s_mod, s_gs1 = [sem(n) for n in (
            "s_csil", "ada_row", "ada_out", "s_mod", "s_gs1")]
        prm_act, prm_dve, row_dve, row_T, chan_ok = [sem(n) for n in ("prm_act", "prm_dve", "row_dve", "row_T", "chan_ok")]
        ct_T, ct_ok, cpad_ok, bp_ok, bp_step, cp_step, cp_ok = [sem(n) for n in (
            "ct_T", "ct_ok", "cpad_ok", "bp_ok", "bp_step", "cp_step", "cp_ok")]
        nrm_xt, nrm_sq, nrm_ms, nrm_rt, nrm_xn, nrm_dve, xT_mm, hT_ok = [sem(n) for n in (
            "nrm_xt", "nrm_sq", "nrm_ms", "nrm_rt", "nrm_xn", "nrm_dve", "xT_mm", "hT_ok")]
        u_mm, u_ok, z_mm, z_ok, kk_mm, kk_act, kk_ok, zero_ok = [sem(n) for n in (
            "u_mm", "u_ok", "z_mm", "z_ok", "kk_mm", "kk_act", "kk_ok", "zero_ok")]

        cond = misc[:, 0:16].rearrange("p (r c) -> p r c", r=2)
        g1n, g2n = misc[:, 16:24], misc[:, 24:32]
        gs1 = misc[:, 32:48].rearrange("p (r c) -> p r c", r=2)
        gs2 = misc[:, 48:64].rearrange("p (r c) -> p r c", r=2)
        dsk = misc[:, 64:70]
        nst = misc[:, 72:96]
        csil = misc[:, 128:384].rearrange("p (c m) -> p c m", m=32)
        tmpc = misc[:, 384:480].rearrange("p (a n) -> p a n", n=DQ)

        rows = at(o_A, 24 * P, slice(0, DQ)).rearrange("p (a n) -> p a n", n=P)
        (LR, LI, XR, TH, KQ, RR, RH, SN, SH, CS, MG, DEN, NRr, T1, T2) = [rows[:, n] for n in range(6, 21)]
        AR, AI, QR, QI, H0R, H0I = [rows[:, n] for n in range(6)]
        LD, DT = rows[:, 21, 0:2], rows[:, 21, 4:6]
        CL = at(o_A + 3072, 12 * P).rearrange("p (f n) -> p f n", n=P)
        BL = at(o_V, 1536).rearrange("p (r n h) -> p r n h", r=2, h=GH)
        CT = at(o_V + 1536, 1536).rearrange("p (r n h) -> p r n h", r=2, h=GH)
        Cpad = at(o_V + 3072, 3072).rearrange("p (r n m) -> p r n m", r=2, m=32)
        q_ch = at(o_U + 1536, 96).rearrange("p (r n) -> p r n", r=2)
        bp_tmp = at(o_U, 1536)
        cp_tmp = at(o_S, 768)
        xbuf = at(o_T, 2048).rearrange("p (b n) -> p b n", b=2)
        xsq = at(o_K, D)
        ada_sb = [at(o_Z, 512), at(o_T, 512), at(o_T + 512, 512)]

        def src_cond(name):
            v = i[name]
            v = v.rearrange("(a d) -> a d", a=1) if len(v.shape) == 1 else v
            return v.rearrange("a (p c) -> p (a c)", p=P)

        with nc.Block() as block:
            @block.sync
            def _(sp):
                def load(n):
                    kind, b, c = items[n]
                    if n >= NR:
                        sp.wait_ge(ring_used, n - NR + 1)
                    dst = ring[:, n % NR, :]
                    if kind == "ada" and c < KC:
                        src = i["w_ada"][0].rearrange("(p c) n -> p c n", c=KC)[:, c, 2048 * b:2048 * (b + 1)]
                    elif kind == "ada":
                        dst, src = ring[0:1, n % NR, :], i["b_ada"][:, 2048 * b:2048 * (b + 1)]
                    else:
                        dst = dst.rearrange("p (c n) -> p c n", c=2)
                        src = i["w_in"][0].rearrange("(p c) n -> p c n", c=KC)[:, 2 * c:2 * c + 2, 0:1024]
                    sp.dma_start(dst, src).then_inc(ring_in[n % NR], 16)

                sp.dma_start(const, i["k_const"]).then_inc(s_const, 16)
                sp.dma_start(cond[:, 0], src_cond("c_ctx")).then_inc(s_cond, 16)
                sp.dma_start(cond[:, 1], src_cond("c")).then_inc(s_cond, 16)
                sp.dma_start(LR, i["lam_re"][0].rearrange("d (q a) n -> (d q) (a n)", a=2)).then_inc(s_rows, 16)
                sp.dma_start(LI, i["lam_im"][0].rearrange("d (q a) n -> (d q) (a n)", a=2)).then_inc(s_rows, 16)
                sp.dma_start(LD, i["log_dt"][0].rearrange("d (q a) -> (d q) a", a=2)).then_inc(s_rows, 16)
                sp.dma_start(H0R, i["state_s5_re"][0, 0].rearrange("d (q a) n -> (d q) (a n)", a=2)).then_inc(s_rows, 16)
                sp.dma_start(H0I, i["state_s5_im"][0, 0].rearrange("d (q a) n -> (d q) (a n)", a=2)).then_inc(s_rows, 16)
                for n in range(NR):
                    load(n)
                for n in range(NR, len(items)):
                    load(n)

            @block.gpsimd
            def _(pool):
                for r, name in enumerate(("c_re", "c_im")):
                    v = i[name][0].rearrange("d (f q a) h n -> q a h (d f) n", q=4, a=2)
                    for q in range(4):
                        for a in range(2):
                            pool.dma_start(CL[(r * 4 + q) * GH:(r * 4 + q + 1) * GH, :, a * NS:(a + 1) * NS],
                                           v[q, a]).then_inc(s_c, 16)
                for r, name in enumerate(("b_re", "b_im")):
                    pool.dma_start(BL[:, r], i[name][0].rearrange("d (q a) n h -> (a n) (d q) h", a=2)).then_inc(s_b, 16)
                pool.dma_start(g1n, i["norm1_g"][0].rearrange("(p c) -> p c", c=KC)).then_inc(s_dg, 16)
                pool.dma_start(g2n, i["norm2_g"][0].rearrange("(p c) -> p c", c=KC)).then_inc(s_dg, 16)
                pool.dma_start(dsk, i["d_skip"][0].rearrange("(f p) -> p f", p=P),
                               allow_slow_non_contiguous=True).then_inc(s_dg, 16)
                pool.wait_ge(ct_ok, 3)
                pool.wait_ge(chan_ok, 1)
                steps = 0
                for m in (0, 1, 2, 4):
                    av = a_pow[{0: 0, 1: 0, 2: 1, 4: 2}[m]]
                    w = max(m, 1)
                    for d in range(2):
                        for half in range(2):
                            qs = slice(d * Q + half * 12, d * Q + half * 12 + 12)
                            if m == 0:
                                src = [CT[:, r, qs, :].unsqueeze(2) for r in range(2)]
                                dst = slice(0, 1) if d == 0 else slice(7, 8)
                            elif d == 0:
                                src = [CP[:, r, qs, 0:w, :] for r in range(2)]
                                dst = slice(w, 2 * w)
                            else:
                                src = [CP[:, r, qs, 8 - w:8, :] for r in range(2)]
                                dst = slice(8 - 2 * w, 8 - w)
                            flat = lambda v: v.rearrange("p n s h -> p n (s h)")
                            src = [flat(v) for v in src]
                            outs = [flat(CP[:, r, qs, dst, :]) for r in range(2)]
                            t = cp_tmp[:, 0:12 * w * GH].rearrange("p (n k) -> p n k", n=12)
                            ar, ai = [av[:, r, qs].unsqueeze(2).to_broadcast([P, 12, w * GH]) for r in range(2)]
                            for (x1, x2, op, dest) in ((0, 1, ALU.add, outs[0]), (1, 0, ALU.subtract, outs[1])):
                                if steps:
                                    pool.wait_ge(cp_step, steps)
                                pool.tensor_tensor(t, src[x2], ai, ALU.mult)
                                pool.tensor_tensor(dest, src[x1], ar, ALU.mult).then_inc(cp_step, 1)
                                steps += 1
                                pool.wait_ge(cp_step, steps)
                                pool.tensor_tensor(dest, dest, t, op).then_inc(cp_step, 1)
                                steps += 1

            @block.scalar
            def _(act):
                def x_tile(j):
                    if j == 2:
                        act.wait_ge(xT_mm, 2)
                    src = i["x_prompt"][0] if j == 0 else i["x_sample"][0, (j - 1) * P:j * P, :]
                    act.dma_start(xbuf[:, j % 2, :], src).then_inc(s_x[j], 16)

                def squares(j):
                    act.wait_ge(nrm_xt, j + 1)
                    if j:
                        act.wait_ge(nrm_sq, j)
                    nc.scalar.activation(xsq, xbuf[:, j % 2, :], ACT.Square, accum_out=nst[:, j:j + 1]).then_inc(nrm_sq, 1)
                    act.wait_ge(nrm_ms, j + 1)
                    nc.scalar.activation(nst[:, 8 + j:9 + j], nst[:, 4 + j:5 + j], ACT.Sqrt).then_inc(nrm_rt, 1)

                x_tile(0)
                x_tile(1)
                act.dma_start(at(o_H, D), i["k_pos"][0:P, :]).then_inc(s_pos[0], 16)
                act.dma_start(at(o_H + D, D), i["k_pos"][P:2 * P, :]).then_inc(s_pos[1], 16)
                act.wait_ge(zero_ok, 1)
                act.wait_ge(s_cond, 32)
                for r in range(2):
                    nc.scalar.activation(csil[:, :, r], cond[:, r], ACT.Silu).then_inc(s_csil, 1)
                act.wait_ge(s_rows, 80)
                nc.scalar.activation(DT, LD, ACT.Exp).then_inc(prm_act, 1)
                act.wait_ge(prm_dve, 1)
                nc.scalar.activation(MG, XR, ACT.Exp).then_inc(prm_act, 1)
                act.wait_ge(prm_dve, 2)
                nc.scalar.activation(SN, RR, ACT.Sin).then_inc(prm_act, 1)
                nc.scalar.activation(SH, RH, ACT.Sin).then_inc(prm_act, 1)
                squares(0)
                squares(1)
                for f in range(3):
                    act.wait_ge(ct_T, f + 1)
                    for k in range(4):
                        for r in range(2):
                            n = (4 * f + k) * 4
                            ins = nc.scalar.activation(
                                CT[:, r, n:n + 4, :].rearrange("p n h -> p (n h)"),
                                bank[f][:, k * P + r * 64:k * P + r * 64 + 64], ACT.Copy, scale=1.0 if r == 0 else -1.0)
                    ins.then_inc(ct_ok, 1)

                def ada_rows(b):
                    act.wait_ge(ring_used, where["ada", b, KC] + 1)
                    nc.scalar.activation(ada_sb[b], bank[0][:, :], ACT.Copy).then_inc(ada_row, 1)
                    act.wait_ge(ada_row, b + 1)
                    for j in range(4):
                        n = 2048 * b + 512 * j
                        act.dma_start(ada_dram[:, n:n + 512], ada_sb[b][32 * j:32 * j + 2, :]).then_inc(ada_out, 16)

                ada_rows(0)
                act.wait_ge(ada_out, 64)
                for r in range(2):
                    act.dma_start(mod[:, r, 0:2, :], ada_dram[r, 0:2 * D].rearrange("(m p c) -> p m c", m=2, c=KC)
                                  ).then_inc(s_mod, 16)
                x_tile(2)
                squares(2)
                act.wait_ge(s_gs1, 1)
                for j in range(NT):
                    r = 0 if j == 0 else 1
                    for h in range(2):
                        act.wait_ge(xT_mm, 2 * j + h + 1)
                        for c in range(4):
                            cc = 4 * h + c
                            ins = nc.scalar.activation(hT[:, cc, j * P:(j + 1) * P], bank[1 + h][:, c * P:(c + 1) * P],
                                                       ACT.Identity, scale=gs1[:, r, cc:cc + 1], bias=mod[:, r, 0, cc:cc + 1])
                        ins.then_inc(hT_ok, 1)
                act.wait_ge(bp_ok, 2)
                for f in range(FT):
                    act.wait_ge(u_mm, f + 1)
                    nc.scalar.activation(uT[:, f, :], bank[3 + f % 2][:, 0:TOK], ACT.Copy).then_inc(u_ok, 1)
                for j in range(NT):
                    if j < NT - 1:
                        act.wait_ge(z_mm, j + 1)
                    else:
                        act.wait_ge(ring_used, KC + 1 + 4)
                    nc.scalar.activation(Z[:, j, :], bank[5 + j % 2][:, 0:DF], ACT.Copy).then_inc(z_ok, 1)
                ada_rows(1)
                ada_rows(2)
                for f in range(FT):
                    act.wait_ge(kk_mm, f + 1)
                    w = (LC - 1) * GH
                    nc.scalar.activation(KK[:, f, 0:w], bank[6 + f % 2][:, 0:w], ACT.Copy)
                    nc.scalar.activation(KK[:, f, w + GH:KW], bank[6 + f % 2][:, w + GH:KW], ACT.Copy).then_inc(kk_act, 1)
                act.wait_ge(ada_out, 192)

            @block.tensor
            def _(pe):
                pe.wait_ge(s_const, 16)
                pe.wait_ge(s_c, 256)
                for f in range(3):
                    for k in range(4):
                        ins = nc.tensor.transpose(bank[f][:, k * P:(k + 1) * P], CL[:, 4 * f + k, :], ident)
                    ins.then_inc(ct_T, 1)
                pe.wait_ge(row_dve, 1)
                for k in range(6):
                    ins = nc.tensor.transpose(bank[7][:, k * DQ:(k + 1) * DQ], rows[:, k], ident[0:DQ, 0:DQ])
                ins.then_inc(row_T, 1)

                def arrived(it):
                    n = where[it]
                    pe.wait_ge(ring_in[n % NR], 16 * (n // NR + 1))
                    return ring[:, n % NR, :]

                def ada(b):
                    if b == 0:
                        pe.wait_ge(ct_ok, 1)
                    else:
                        pe.wait_ge(ada_row, b)
                    for c in range(KC + 1):
                        w = arrived(("ada", b, c))
                        if c == 0 and b == 0:
                            pe.wait_ge(s_csil, 2)
                        for j in range(4):
                            lhs = csil[:, c, :] if c < KC else const[0:1, C_ONE:C_ONE + 32]
                            rhs = w[:, 512 * j:512 * j + 512] if c < KC else w[0:1, 512 * j:512 * j + 512]
                            ins = nc.tensor.matmul(bank[0][32 * j:32 * j + 32, :], lhs, rhs, start=c == 0, stop=c == KC)
                        ins.then_inc(ring_used, 1)

                pe.wait_ge(chan_ok, 1)
                ada(0)
                for j in range(NT):
                    pe.wait_ge(nrm_xn, j + 1)
                    for h in range(2):
                        if j == 0:
                            pe.wait_ge(ct_ok, 2 + h)
                        else:
                            pe.wait_ge(hT_ok, 2 * (j - 1) + h + 1)
                        for c in range(4):
                            ins = nc.tensor.transpose(bank[1 + h][:, c * P:(c + 1) * P],
                                                      xbuf[:, j % 2, 4 * h + c:D:KC], ident)
                        ins.then_inc(xT_mm, 1)
                w_a = [arrived(("in", 0, c // 2)).rearrange("p (c n) -> p c n", c=2)[:, c % 2] for c in range(KC)]
                pe.wait_ge(hT_ok, 6)
                for f in range(FT):
                    if f >= 2:
                        pe.wait_ge(u_ok, f - 1)
                    for c in range(KC):
                        ins = nc.tensor.matmul(bank[3 + f % 2][:, 0:TOK], w_a[c][:, f * P:(f + 1) * P], hT[:, c, :],
                                               start=c == 0, stop=c == KC - 1)
                    ins.then_inc(u_mm, 1)
                for j in range(NT):
                    if j >= 2:
                        pe.wait_ge(z_ok, j - 1)
                    for c in range(KC):
                        ins = nc.tensor.matmul(bank[5 + j % 2][:, 0:DF], hT[:, c, j * P:(j + 1) * P], w_a[c][:, DS:DS + DF],
                                               start=c == 0, stop=c == KC - 1)
                    if j < NT - 1:
                        ins.then_inc(z_mm, 1)
                    else:
                        ins.then_inc(ring_used, 4)
                ada(1)
                ada(2)
                pe.wait_ge(cpad_ok, 2)
                pe.wait_ge(bp_ok, 2)
                for f in range(FT):
                    if f >= 2:
                        pe.wait_ge(kk_ok, f - 1)
                    elif f == 0:
                        pe.wait_ge(z_ok, 3)
                    for q in range(4):
                        for n, (d, r) in enumerate(((0, 0), (0, 1), (1, 0), (1, 1))):
                            dq = d * Q + 4 * f + q
                            c0 = 0 if d == 0 else (LC - 1) * GH
                            ins = nc.tensor.matmul(bank[6 + f % 2][32 * q:32 * q + 32, c0:c0 + P], Cpad[:, r, dq, :],
                                                   BP[:, r, dq].rearrange("p s h -> p (s h)"),
                                                   start=n == 0, stop=n == 3, skip_group_check=True)
                    ins.then_inc(kk_mm, 1)

            @block.vector
            def _(dve):
                def step(ins):
                    n_step[0] += 1
                    ins.then_inc(dve_step, 1)
                    dve.wait_ge(dve_step, n_step[0])

                tt = nc.vector.tensor_tensor
                ts = nc.vector.tensor_scalar
                stt = nc.vector.scalar_tensor_tensor
                nc.vector.memset(csil[:, :, :], 0.0).then_inc(zero_ok, 1)
                dve.wait_ge(s_rows, 80)
                step(ts(LR, LR, -1e-4, None, ALU.min))
                dve.wait_ge(prm_act, 1)
                for a in range(2):
                    cols = slice(a * NS, (a + 1) * NS)
                    ts(TH[:, cols], LI[:, cols], DT[:, a:a + 1], None, ALU.mult)
                    ins = ts(XR[:, cols], LR[:, cols], DT[:, a:a + 1], None, ALU.mult)
                ins.then_inc(prm_dve, 1)
                dve.wait_ge(prm_dve, 1)
                step(ts(KQ, TH, 1.0 / (2 * np.pi), MAGIC, ALU.mult, ALU.add))
                step(ts(KQ, KQ, MAGIC, None, ALU.subtract))
                step(stt(out=RR, in0=KQ, scalar=-PI_A, in1=TH, op0=ALU.mult, op1=ALU.add))
                step(stt(out=RR, in0=KQ, scalar=-PI_B, in1=RR, op0=ALU.mult, op1=ALU.add))
                step(stt(out=RR, in0=KQ, scalar=-PI_C, in1=RR, op0=ALU.mult, op1=ALU.add))
                step(ts(RR, RR, 3.1415925, -3.1415925, ALU.min, ALU.max))
                ts(RH, RR, 0.5, None, ALU.mult).then_inc(prm_dve, 1)
                tt(DEN, LR, LR, ALU.mult)
                step(tt(T1, LI, LI, ALU.mult))
                step(tt(DEN, DEN, T1, ALU.add))
                step(nc.vector.reciprocal(DEN, DEN))
                dve.wait_ge(prm_act, 4)
                step(tt(CS, SH, SH, ALU.mult))
                step(ts(CS, CS, -2.0, 1.0, ALU.mult, ALU.add))
                tt(AI, MG, SN, ALU.mult)
                step(tt(AR, MG, CS, ALU.mult))
                step(ts(NRr, AR, 1.0, None, ALU.subtract))
                tt(T1, AI, LI, ALU.mult)
                step(tt(T2, NRr, LR, ALU.mult))
                step(tt(T1, T1, T2, ALU.add))
                step(tt(QR, T1, DEN, ALU.mult))
                tt(T1, AI, LR, ALU.mult)
                step(tt(T2, NRr, LI, ALU.mult))
                step(tt(T1, T1, T2, ALU.subtract))
                tt(QI, T1, DEN, ALU.mult).then_inc(row_dve, 1)
                dve.wait_ge(row_T, 1)
                rt = bank[7][:, 0:6 * DQ].rearrange("p (a n) -> p a n", n=DQ)
                nc.vector.tensor_copy(a_pow[0], rt[:, 0:2])
                nc.vector.tensor_copy(q_ch, rt[:, 2:4])
                step(nc.vector.tensor_copy(h0, rt[:, 4:6]))
                for k in range(3):
                    x = a_pow[k]
                    tt(tmpc[:, 0], x[:, 0], x[:, 0], ALU.mult)
                    tt(tmpc[:, 1], x[:, 1], x[:, 1], ALU.mult)
                    if k < 2:
                        step(stt(out=a_pow[k + 1][:, 1], in0=x[:, 0], scalar=2.0, in1=x[:, 1], op0=ALU.mult, op1=ALU.mult))
                        step(tt(a_pow[k + 1][:, 0], tmpc[:, 0], tmpc[:, 1], ALU.subtract))
                    else:
                        stt(out=Aii[:, 0], in0=x[:, 0], scalar=-2.0, in1=x[:, 1], op0=ALU.mult, op1=ALU.mult)
                        step(stt(out=Aii[:, 1], in0=x[:, 0], scalar=2.0, in1=x[:, 1], op0=ALU.mult, op1=ALU.mult))
                        tt(Arr[:, 0], tmpc[:, 0], tmpc[:, 1], ALU.subtract)
                        step(tt(Arr[:, 1], tmpc[:, 0], tmpc[:, 1], ALU.subtract))
                nc.vector.tensor_copy(tmpc[:, 0, 0:1], tmpc[:, 0, 1:2]).then_inc(chan_ok, 1)

                def norm(j):
                    dve.wait_ge(s_x[j], 16)
                    x = xbuf[:, j % 2, :]
                    if j:
                        dve.wait_ge(s_pos[j - 1], 16)
                        tt(x, x, at(o_H + (j - 1) * D, D), ALU.add).then_inc(nrm_xt, 1)
                    else:
                        ts(nst[:, 23:24], x[:, 0:1], 1.0, None, ALU.mult).then_inc(nrm_xt, 1)
                    dve.wait_ge(nrm_sq, j + 1)
                    ts(nst[:, 4 + j:5 + j], nst[:, j:j + 1], 1.0 / D, EPS, ALU.mult, ALU.add).then_inc(nrm_ms, 1)
                    dve.wait_ge(nrm_rt, j + 1)
                    step(nc.vector.reciprocal(nst[:, 12 + j:13 + j], nst[:, 8 + j:9 + j]))
                    ts(x, x, nst[:, 12 + j:13 + j], None, ALU.mult).then_inc(nrm_xn, 1)

                norm(0)
                norm(1)
                dve.wait_ge(ct_ok, 3)
                for r in range(2):
                    tt(Cpad[:, r].rearrange("p n (a h) -> p n a h", a=2),
                       CT[:, r].unsqueeze(2).to_broadcast([P, DQ, 2, GH]),
                       const[:, C_PAR:C_PAR + 32].rearrange("p (a h) -> p a h", a=2).unsqueeze(1).to_broadcast([P, DQ, 2, GH]),
                       ALU.mult).then_inc(cpad_ok, 1)
                dve.wait_ge(s_b, 32)
                flat = lambda v: v.rearrange("p n s h -> p n (s h)")

                def bp_level(d, m):
                    w = max(m, 1)
                    qs = slice(d * Q, (d + 1) * Q)
                    if m == 0:
                        src = [BL[:, r, qs, :] for r in range(2)]
                        dst = slice(7, 8) if d == 0 else slice(0, 1)
                        av = q_ch
                    else:
                        av = a_pow[{1: 0, 2: 1, 4: 2}[m]]
                        src = [flat(BP[:, r, qs, 8 - w:8, :] if d == 0 else BP[:, r, qs, 0:w, :]) for r in range(2)]
                        dst = slice(8 - 2 * w, 8 - w) if d == 0 else slice(w, 2 * w)
                    outs = [flat(BP[:, r, qs, dst, :]) for r in range(2)]
                    t = bp_tmp[:, 0:Q * w * GH].rearrange("p (n k) -> p n k", n=Q)
                    ar, ai = [av[:, r, qs].unsqueeze(2).to_broadcast([P, Q, w * GH]) for r in range(2)]
                    for (x1, x2, op, dest) in ((0, 1, ALU.subtract, outs[0]), (1, 0, ALU.add, outs[1])):
                        tt(t, src[x2], ai, ALU.mult)
                        step(tt(dest, src[x1], ar, ALU.mult))
                        step(tt(dest, dest, t, op))

                for m in (0, 1, 2, 4):
                    bp_level(0, m)
                norm(2)
                dve.wait_ge(s_mod, 32)
                dve.wait_ge(s_dg, 48)
                for r in range(2):
                    ins = stt(out=gs1[:, r], in0=mod[:, r, 1, :], scalar=1.0, in1=g1n, op0=ALU.add, op1=ALU.mult)
                ins.then_inc(s_gs1, 1)
                for m in (0, 1, 2, 4):
                    bp_level(1, m)
                nc.vector.tensor_copy(tmpc[:, 0, 0:1], tmpc[:, 0, 1:2]).then_inc(bp_ok, 2)
                for f in range(FT):
                    dve.wait_ge(kk_act, f + 1)
                    w = (LC - 1) * GH
                    stt(out=KK[:, f, w:w + GH], in0=const[:, C_M16:C_M16 + GH], scalar=dsk[:, f:f + 1],
                        in1=bank[6 + f % 2][:, w:w + GH], op0=ALU.mult, op1=ALU.add).then_inc(kk_ok, 1)

        Uc = at(o_V, LC * DS, slice(0, NC))
        U = at(o_U, G * NC).rearrange("p (g k) -> p g k", g=G)
        V = at(o_V, 2 * DQ * NC).rearrange("p (r n k) -> p r n k", r=2, n=DQ)
        GLT = at(o_A, 16 * TOK).rearrange("p (m t) -> p m t", m=16)
        Sin = at(o_A + 6144, 2 * DQ * NC).rearrange("p (r n k) -> p r n k", r=2, n=DQ)
        Srev = at(o_S, 768).rearrange("p (b r n k) -> p b r n k", b=2, r=2, n=4)
        BT = at(o_T, 2048).rearrange("p (s x n) -> p s x n", s=4, x=4)
        Tt = at(o_T, 2048).rearrange("p (b g t h) -> p b g t h", b=2, g=8, h=GH)
        Yc = at(o_V, LC * DS, slice(0, NC)).rearrange("p (t f) -> p t f", t=LC)
        fin = misc[:, 128:224].rearrange("p (r n) -> p r n", r=2)
        fin_rows = [at(o_ch + P * r, P, slice(0, DQ)) for r in range(2)]
        t1, t2 = [misc[:, 224 + 96 * k:320 + 96 * k].rearrange("p (r n) -> p r n", r=2) for k in range(2)]
        t3 = misc[:, 416:512].rearrange("p (r n) -> p r n", r=2)
        gate_in = [sem(f"gate_in{n}") for n in range(NR)]
        uc_T, uc_ok, u2_T, u2_ok, bt_T, bt_ok, v_mm, v_ok, scan_ok, fin_ok, fin_T, fin_row, dram_out = [sem(n) for n in (
            "uc_T", "uc_ok", "u2_T", "u2_ok", "bt_T", "bt_ok", "v_mm", "v_ok", "scan_ok", "fin_ok", "fin_T", "fin_row", "dram_out")]
        gl_mm, gl_ok, t_T, t_ok, srev_ok, y_mm, y_ok = [sem(n) for n in (
            "gl_mm", "gl_ok", "t_T", "t_ok", "srev_ok", "y_mm", "y_ok")]
        w_glu = at(o_W, FT * DS).rearrange("p (k n) -> p k n", k=FT)
        w_p5 = at(o_W + FT * DS, 5 * D).rearrange("p (k n) -> p k n", k=5)
        glu_in, p5_in = sem("glu_in"), sem("p5_in")
        NUC = LC * FT // 4

        def uc_copy(b):
            f, half = divmod(b, 2)
            dst = Uc[:, D * f:D * f + D].rearrange("p (g s h) -> p s g h", g=8, h=GH)[:, 4 * half:4 * half + 4]
            return dst, bank[b % 2][0:NC, :].rearrange("p (s g h) -> p s g h", s=4, h=GH)

        with nc.Block() as block:
            @block.sync
            def _(sp):
                for n in range(8):
                    if n >= NR:
                        sp.wait_ge(gl_mm, 2 * (n - NR) + 2)
                    sp.dma_start(ring[:, n % NR, :].rearrange("p (c n) -> p c n", c=KC),
                                 i["w_in"][0].rearrange("(p c) n -> p c n", c=KC)[:, :, 1024 + 256 * n:1280 + 256 * n]
                                 ).then_inc(gate_in[n % NR], 16)
                sp.wait_ge(gl_mm, 16)
                sp.dma_start(w_glu, i["w_glu"][0].rearrange("(k p) n -> p k n", p=P)).then_inc(glu_in, 16)
                sp.dma_start(w_p5, i["w_proj_s5"][0, 0:5 * P, :].rearrange("(k p) n -> p k n", p=P)).then_inc(p5_in, 16)
                sp.wait_ge(fin_row, 2)
                sp.dma_start(o["st_re"][0, 0].rearrange("d (q a) n -> (d q) (a n)", a=2), fin_rows[0]
                             ).then_inc(dram_out, 16)
                sp.dma_start(o["st_im"][0, 0].rearrange("d (q a) n -> (d q) (a n)", a=2), fin_rows[1]
                             ).then_inc(dram_out, 16)
                sp.wait_ge(dram_out, 32)

            @block.tensor
            def _(pe):
                for b in range(NUC):
                    if b >= 2:
                        pe.wait_ge(uc_ok, b - 1)
                    for k in range(4):
                        f, s = divmod(4 * b + k, LC)
                        ins = nc.tensor.transpose(bank[b % 2][0:NC, k * P:(k + 1) * P], uT[:, f, s:TOK:LC], ident)
                    ins.then_inc(uc_T, 1)
                pe.wait_ge(uc_ok, NUC)
                for b in range(6):
                    if b >= 2:
                        pe.wait_ge(u2_ok, b - 1)
                    for k in range(8):
                        ins = nc.tensor.transpose(bank[2 + b % 2][:, k * NC:(k + 1) * NC], Uc[:, P * (8 * b + k):P * (8 * b + k) + P],
                                                  ident[0:NC, 0:NC])
                    ins.then_inc(u2_T, 1)

                def bt(q):
                    if q >= 2:
                        pe.wait_ge(bt_ok, q - 1)
                    for x in range(4):
                        d, r = divmod(x, 2)
                        ins = nc.tensor.transpose(bank[4 + q % 2][:, x * P:(x + 1) * P],
                                                  BP[:, r, d * Q + q].rearrange("p s h -> p (s h)"), ident)
                    ins.then_inc(bt_T, 1)

                def sums(q):
                    pe.wait_ge(bt_ok, q + 1)
                    if q >= 2:
                        pe.wait_ge(v_ok, q - 1)
                    if q == 0:
                        pe.wait_ge(u2_ok, 6)
                    for x in range(4):
                        for a in range(2):
                            ins = nc.tensor.matmul(bank[6 + q % 2][64 * a:64 * a + 64, x * NC:(x + 1) * NC],
                                                   BT[:, q % 4, x, 64 * a:64 * a + 64], U[:, 2 * q + a, :],
                                                   start=True, stop=True)
                    ins.then_inc(v_mm, 1)

                bt(0)
                for q in range(Q):
                    if q + 1 < Q:
                        bt(q + 1)
                    sums(q)
                for m in range(16):
                    n = m // 2
                    pe.wait_ge(gate_in[n % NR], 16 * (n // NR + 1))
                    if m >= 2:
                        pe.wait_ge(gl_ok, m - 1)
                    w = ring[:, n % NR, :].rearrange("p (c n) -> p c n", c=KC)
                    for c in range(KC):
                        ins = nc.tensor.matmul(bank[m % 2][:, 0:TOK], w[:, c, P * (m % 2):P * (m % 2) + P], hT[:, c, :],
                                               start=c == 0, stop=c == KC - 1)
                    ins.then_inc(gl_mm, 1)
                pe.wait_ge(fin_ok, 1)
                for r in range(2):
                    ins = nc.tensor.transpose(bank[2][0:DQ, r * P:(r + 1) * P], fin[:, r], ident)
                ins.then_inc(fin_T, 1)

                def kernels(f):
                    for half in range(2):
                        if f >= 1:
                            pe.wait_ge(t_ok, 2 * (f - 1) + half + 1)
                        for k in range(4):
                            t = 4 * half + k
                            c0 = GH * (LC - 1 - t)
                            ins = nc.tensor.transpose(bank[4 + half][:, k * P:(k + 1) * P], KK[:, f, c0:c0 + P], ident)
                        ins.then_inc(t_T, 1)

                def outputs(f):
                    pe.wait_ge(t_ok, 2 * f + 2)
                    pe.wait_ge(srev_ok, f + 1)
                    if f == 0:
                        pe.wait_ge(scan_ok, 2)
                    if f >= 2:
                        pe.wait_ge(y_ok, f - 1)
                    for q4 in range(4):
                        q = 4 * f + q4
                        out = [bank[6 + f % 2][64 * a:64 * a + NC, P * q4:P * q4 + P] for a in range(2)]
                        for a in range(2):
                            nc.tensor.matmul(out[a], U[:, 2 * q + a, :],
                                             Tt[:, f % 2, 2 * q4 + a].rearrange("p t h -> p (t h)"), start=True, stop=False)
                        for n, (d, r) in enumerate(((0, 0), (0, 1), (1, 0), (1, 1))):
                            for a in range(2):
                                rows_ = slice(64 * a, 64 * a + 64)
                                st = Sin[rows_, r, q, :] if d == 0 else Srev[rows_, f % 2, r, q4, :]
                                ins = nc.tensor.matmul(out[a], st, CP[rows_, r, d * Q + q].rearrange("p t h -> p (t h)"),
                                                       start=False, stop=n == 3)
                    ins.then_inc(y_mm, 1)

                kernels(0)
                for f in range(FT):
                    if f + 1 < FT:
                        kernels(f + 1)
                    outputs(f)

            @block.scalar
            def _(act):
                for b in range(0, NUC, 2):
                    act.wait_ge(uc_T, b + 1)
                    if b:
                        act.wait_ge(uc_ok, b)
                    nc.scalar.activation(*uc_copy(b), ACT.Copy).then_inc(uc_ok, 1)
                for b in range(6):
                    act.wait_ge(u2_T, b + 1)
                    nc.scalar.activation(U[:, 8 * b:8 * b + 8, :].rearrange("p g k -> p (g k)"), bank[2 + b % 2][:, 0:8 * NC],
                                         ACT.Copy).then_inc(u2_ok, 1)
                for q in range(Q):
                    act.wait_ge(bt_T, q + 1)
                    if q >= 4:
                        act.wait_ge(v_mm, q - 3)
                    nc.scalar.activation(BT[:, q % 4].rearrange("p x n -> p (x n)"), bank[4 + q % 2][:, :], ACT.Copy
                                         ).then_inc(bt_ok, 1)
                for m in range(16):
                    act.wait_ge(gl_mm, m + 1)
                    nc.scalar.activation(GLT[:, m, :], bank[m % 2][:, 0:TOK], ACT.Sigmoid).then_inc(gl_ok, 1)
                act.wait_ge(fin_T, 1)
                for r in range(2):
                    nc.scalar.activation(fin_rows[r], bank[2][0:DQ, r * P:(r + 1) * P],
                                         ACT.Copy).then_inc(fin_row, 1)
                act.wait_ge(scan_ok, 2)
                for f in range(FT):
                    if f >= 2:
                        act.wait_ge(y_mm, f - 1)
                    nc.scalar.activation(Srev[:, f % 2], Sin[:, :, Q + 4 * f:Q + 4 * f + 4, ::-1], ACT.Copy).then_inc(srev_ok, 1)
                    act.wait_ge(t_T, 2 * f + 1)
                    if f >= 2:
                        act.wait_ge(y_mm, f - 1)
                    nc.scalar.activation(Tt[:, f % 2, :, 0:4, :].rearrange("p g t h -> p t g h"),
                                         bank[4][:, :].rearrange("p (t g h) -> p t g h", t=4, h=GH), ACT.Copy).then_inc(t_ok, 1)
                    act.wait_ge(t_T, 2 * f + 2)
                    nc.scalar.activation(Tt[:, f % 2, :, 4:8, :].rearrange("p g t h -> p t g h"),
                                         bank[5][:, :].rearrange("p (t g h) -> p t g h", t=4, h=GH), ACT.Copy).then_inc(t_ok, 1)

            @block.vector
            def _(dve):
                scan_c, scan_l = sem("scan_c"), sem("scan_l")
                tt = nc.vector.tensor_tensor
                for b in range(1, NUC, 2):
                    dve.wait_ge(uc_T, b + 1)
                    dve.wait_ge(uc_ok, b)
                    nc.vector.tensor_copy(*uc_copy(b)).then_inc(uc_ok, 1)
                for q in range(Q):
                    dve.wait_ge(v_mm, q + 1)
                    ps = bank[6 + q % 2][:, 0:4 * NC].rearrange("p (d r k) -> p d r k", d=2, r=2)
                    nc.vector.tensor_copy(V[:, :, q, :], ps[:, 0])
                    nc.vector.tensor_copy(V[:, :, Q + q, :], ps[:, 1, :, ::-1]).then_inc(v_ok, 1)
                dve.wait_ge(v_ok, Q)
                S4 = Sin.rearrange("p r (d q) k -> p r d q k", d=2)
                V4 = V.rearrange("p r (d q) k -> p r d q k", d=2)

                def cols(v, ctx_seq, j):
                    f, b = (j, CC * 2 + j) if ctx_seq else (CC + j, j)
                    return v[:, :, 0, :, f], v[:, :, 1, :, b]

                h04 = h0.rearrange("p r (d q) -> p r d q", d=2)
                for d, (c, l) in enumerate(zip(cols(S4, True, 0), cols(S4, False, 0))):
                    nc.vector.memset(c, 0.0)
                    nc.vector.tensor_copy(l, h04[:, :, d]).then_inc(scan_l, 1)
                nc.vector.memset(fin, 0.0).then_inc(scan_c, 1)
                nc.vector.tensor_copy(t3, h0).then_inc(scan_l, 1)
                state = {True: fin, False: t3}
                n_c, n_l = 1, 3
                for j in range(32):
                    for ctx_seq in (True, False):
                        if ctx_seq and j >= CC or not ctx_seq and j == 31:
                            continue
                        s, x, sm = state[ctx_seq], (t1 if ctx_seq else t2), (scan_c if ctx_seq else scan_l)
                        n = n_c if ctx_seq else n_l
                        dve.wait_ge(sm, n)
                        tt(x, Aii, s[:, ::-1, :], ALU.mult).then_inc(sm, 1)
                        dve.wait_ge(sm, n + 1)
                        tt(s, Arr, s, ALU.mult).then_inc(sm, 1)
                        xv = x.rearrange("p r (d q) -> p r d q", d=2)
                        vf, vb = cols(V4, ctx_seq, j)
                        tt(xv[:, :, 0], xv[:, :, 0], vf, ALU.add)
                        tt(xv[:, :, 1], xv[:, :, 1], vb, ALU.add).then_inc(sm, 1)
                        dve.wait_ge(sm, n + 3)
                        last = ctx_seq and j == CC - 1
                        tt(s, s, x, ALU.add).then_inc(fin_ok if last else sm, 1)
                        if not last:
                            dve.wait_ge(sm, n + 4)
                            sv = s.rearrange("p r (d q) -> p r d q", d=2)
                            tf, tb = cols(S4, ctx_seq, j + 1)
                            nc.vector.tensor_copy(tf, sv[:, :, 0])
                            ins = nc.vector.tensor_copy(tb, sv[:, :, 1])
                            if not ctx_seq and j == 30:
                                ins.then_inc(scan_ok, 2)
                        if ctx_seq:
                            n_c += 4
                        else:
                            n_l += 4
                for f in range(FT):
                    dve.wait_ge(y_mm, f + 1)
                    for a in range(2):
                        ins = nc.vector.tensor_copy(
                            Yc[:, :, P * f:P * f + P].rearrange("p t (q a h) -> p t q a h", q=4, a=2)[:, :, :, a, :].rearrange("p t q h -> p q t h"),
                            bank[6 + f % 2][64 * a:64 * a + NC, :].rearrange("p (q t h) -> p q t h", q=4, h=GH))
                    ins.then_inc(y_ok, 1)

        w_p6 = at(o_T, D)
        w_pf = at(o_B, 2 * D).rearrange("p (k n) -> p k n", k=2)
        w_o = at(o_B + 2 * D, KC * D).rearrange("p (k n) -> p k n", k=KC)
        dft = at(o_B + 10 * D, N_DFT)
        gT = at(o_U, FT * TOK).rearrange("p (f t) -> p f t", f=FT)
        AT = at(o_H, FT * TOK).rearrange("p (f t) -> p f t", f=FT)
        yfT = at(o_H + FT * TOK, 2 * TOK).rearrange("p (f t) -> p f t", f=2)
        PQ = at(o_V, 4 * TOK).rearrange("p (f x t) -> p f x t", f=2, x=2)
        sgl = at(o_T + D, 2 * TOK).rearrange("p (b t) -> p b t", b=2)
        pos_t = at(o_V + 2048, 2048).rearrange("p (j n) -> p j n", j=2)
        g2g_b = at(o_V + 4096, D)
        x_new = at(o_V, D).rearrange("p (b n) -> p b n", b=2)
        hs = at(o_W + 3072, 2 * TOK).rearrange("p (f t) -> p f t", f=2)
        X = at(o_W, NT * D).rearrange("p (j n) -> p j n", j=NT)
        H = at(o_V, NT * D).rearrange("p (j n) -> p j n", j=NT)
        ACC = at(o_V + 4096, NT * D).rearrange("p (j n) -> p j n", j=NT)
        xn = ACC
        g1b, gs2b, sh2b = [at(o_A + 6144 + 2048 * k, 2048).rearrange("p (r n) -> p r n", r=2) for k in range(3)]
        w_r = at(o_ch, KC * E).rearrange("p (c e) -> p c e", c=KC)
        w_s1, w_s3 = [at(b, 2048).rearrange("p (c n) -> p c n", c=KC) for b in (o_B, o_B + 10 * D)]
        w_s2 = at(o_T, 2048).rearrange("p (c n) -> p c n", c=2)
        lgT = at(o_U, TOK, slice(0, E))
        (sc, bi, mx, msk, th8, gtm, eqm, cum, tmpE) = [at(o_U + TOK + 192 * k, 192) for k in range(9)]
        bias_b = at(o_misc + 128, E)
        gsc, rnk, gm, gneg = [misc[:, 192 + 24 * k:216 + 24 * k] for k in range(4)]
        ngt, lim, wsum, wrec = [misc[:, 288 + 4 * k:291 + 4 * k] for k in range(4)]
        posM, GT, cnt, MS = [at(o_K + 2304 + 192 * k, n) for k, n in enumerate((192, 192, 64))] + [at(o_S + 768 - 192, 192)]
        by_tile = lambda v: v.rearrange("p (j e) -> p j e", j=NT)

        (w3_in, dft_in, x2_in, pos2_in, bc_in, wr_in, ws_in, ws2_in) = [sem(n) for n in (
            "w3_in", "dft_in", "x2_in", "pos2_in", "bc_in", "wr_in", "ws_in", "ws2_in")]
        (g_T, g_ok, f1_mm, f1_ok, f2_mm, f2_ok, glu_mm, glu_sg, glu_ok, pr_mm, pr_ok, o_mm, x2_ok) = [sem(n) for n in (
            "g_T", "g_ok", "f1_mm", "f1_ok", "f2_mm", "f2_ok", "glu_mm", "glu_sg", "glu_ok", "pr_mm", "pr_ok", "o_mm", "x2_ok")]
        (n2_sq, n2_ms, n2_rt, n2_xn, n2_T, n2_hT, n2_g, H_ok, r_mm, r_sg, r_T, sel_ok, pos_mm, pos_ok) = [sem(n) for n in (
            "n2_sq", "n2_ms", "n2_rt", "n2_xn", "n2_T", "n2_hT", "n2_g", "H_ok", "r_mm", "r_sg", "r_T", "sel_ok", "pos_mm", "pos_ok")]
        (sh_mm, sh_si, sh_ok, sy_mm, sy_ok, xp_ok) = [sem(n) for n in ("sh_mm", "sh_si", "sh_ok", "sy_mm", "sy_ok", "xp_ok")]

        with nc.Block() as block:
            @block.sync
            def _(sp):
                sp.dma_start(w_p6, i["w_proj_s5"][0, 5 * P:6 * P, :]).then_inc(w3_in, 16)
                sp.dma_start(dft, i["k_dft"]).then_inc(dft_in, 16)
                sp.dma_start(w_pf, i["w_proj_f"][0].rearrange("(k p) n -> p k n", p=P)).then_inc(w3_in, 16)
                sp.dma_start(w_o, i["w_out"][0].rearrange("(k p) n -> p k n", p=P)).then_inc(w3_in, 16)
                for r in range(2):
                    for k, mm in enumerate((2, 4, 3)):
                        sp.dma_start((g1b, gs2b, sh2b)[k][:, r, :], ada_dram[r, mm * D:(mm + 1) * D].partition_broadcast(P)
                                     ).then_inc(bc_in, 16)
                    sp.dma_start(mod[:, r, 3:5, :], ada_dram[r, 3 * D:5 * D].rearrange("(m p c) -> p m c", m=2, c=KC)
                                 ).then_inc(bc_in, 16)
                sp.dma_start(bias_b, i["router_bias"][0].partition_broadcast(P)).then_inc(wr_in, 16)
                sp.dma_start(w_r, i["w_router"][0].rearrange("(p c) e -> p c e", c=KC)).then_inc(wr_in, 16)
                sp.wait_ge(g_ok, 6)
                sp.dma_start(g2g_b, i["norm2_g"][0].partition_broadcast(P)).then_inc(bc_in, 16)
                sp.dma_start(pos_t, i["k_pos"].rearrange("(j p) n -> p j n", p=P)).then_inc(pos2_in, 16)
                sp.wait_ge(glu_mm, 6)
                sp.dma_start(X[:, 0], i["x_prompt"][0]).then_inc(x2_in, 16)
                sp.dma_start(X[:, 1:3], i["x_sample"][0].rearrange("(j p) n -> p j n", p=P)).then_inc(x2_in, 16)
                sp.wait_ge(pr_mm, 8)
                sp.dma_start(w_s1, i["ws1"][0].rearrange("(p c) n -> p c n", c=KC)).then_inc(ws_in, 16)
                sp.dma_start(w_s3, i["ws3"][0].rearrange("(p c) n -> p c n", c=KC)).then_inc(ws_in, 16)
                sp.dma_start(w_s2, i["ws2"][0].rearrange("(p c) n -> p c n", c=2)).then_inc(ws2_in, 16)
                sp.wait_ge(x2_ok, 6)
                sp.dma_start(x2_dram, X).then_inc(dram_out, 16)
                sp.wait_ge(dram_out, 48)

            @block.tensor
            def _(pe):
                for f in range(FT):
                    if f >= 2:
                        pe.wait_ge(g_ok, f - 1)
                    for t in range(LC):
                        ins = nc.tensor.transpose(bank[f % 2][:, t * NC:(t + 1) * NC], Yc[:, t, f * P:(f + 1) * P], ident[0:NC, 0:NC])
                    ins.then_inc(g_T, 1)
                pe.wait_ge(dft_in, 16)
                for n in range(4):
                    seq, f = divmod(n, 2)
                    if n >= 2:
                        pe.wait_ge(f1_ok, n - 1)
                    if seq == 0:
                        ins = nc.tensor.matmul(bank[2 + n % 2][:, 0:256], Z[:, 0, f * P:(f + 1) * P], dft[:, F_CTX:F_CTX + 256],
                                               start=True, stop=True)
                    else:
                        for j in range(2):
                            ins = nc.tensor.matmul(bank[2 + n % 2][:, :], Z[:, 1 + j, f * P:(f + 1) * P],
                                                   dft[:, F_LAT + 512 * j:F_LAT + 512 * j + 512], start=j == 0, stop=j == 1)
                    ins.then_inc(f1_mm, 1)
                pe.wait_ge(f1_ok, 4)
                for f in range(2):
                    nc.tensor.matmul(bank[4 + f][:, 0:TOK], dft[:, F_BC:F_BC + P], PQ[:, f, 0, :], start=True, stop=False)
                    nc.tensor.matmul(bank[4 + f][:, 0:TOK], dft[:, F_BS:F_BS + P], PQ[:, f, 1, :], start=False, stop=True
                                     ).then_inc(f2_mm, 1)
                pe.wait_ge(glu_in, 16)
                pe.wait_ge(g_ok, 6)
                for f in range(FT):
                    if f >= 2:
                        pe.wait_ge(glu_sg, f - 1)
                    for k in range(FT):
                        ins = nc.tensor.matmul(bank[6 + f % 2][:, 0:TOK], w_glu[:, k, f * P:(f + 1) * P], gT[:, k, :],
                                               start=k == 0, stop=k == FT - 1)
                    ins.then_inc(glu_mm, 1)
                pe.wait_ge(p5_in, 16)
                pe.wait_ge(w3_in, 48)
                pe.wait_ge(glu_ok, 6)
                pe.wait_ge(f2_ok, 2)
                for m in range(KC):
                    if m >= 2:
                        pe.wait_ge(pr_ok, m - 1)
                    for k in range(FT):
                        w = w_p5[:, k] if k < 5 else w_p6
                        nc.tensor.matmul(bank[m % 2][:, 0:TOK], w[:, m * P:(m + 1) * P], AT[:, k, :], start=k == 0, stop=k == FT - 1)
                    for k in range(2):
                        ins = nc.tensor.matmul(bank[2 + m % 2][:, 0:TOK], w_pf[:, k, m * P:(m + 1) * P], yfT[:, k, :],
                                               start=k == 0, stop=k == 1)
                    ins.then_inc(pr_mm, 1)
                pe.wait_ge(pr_ok, KC)
                for j in range(NT):
                    for n in range(2):
                        if 2 * j + n >= 2:
                            pe.wait_ge(x2_ok, 2 * j + n - 1)
                        for m in range(KC):
                            ins = nc.tensor.matmul(bank[4 + n][:, :], GLT[:, m, j * P:(j + 1) * P], w_o[:, m, 512 * n:512 * n + 512],
                                                   start=m == 0, stop=m == KC - 1)
                        ins.then_inc(o_mm, 1)
                for j in range(NT):
                    pe.wait_ge(n2_xn, j + 1)
                    for h in range(2):
                        if j:
                            pe.wait_ge(n2_hT, 2 * (j - 1) + h + 1)
                        for c in range(4):
                            ins = nc.tensor.transpose(bank[6 + h][:, c * P:(c + 1) * P], xn[:, j, 4 * h + c:D:KC], ident)
                        ins.then_inc(n2_T, 1)
                pe.wait_ge(n2_hT, 6)
                pe.wait_ge(wr_in, 32)
                for c in range(KC):
                    ins = nc.tensor.matmul(bank[0][0:E, 0:TOK], w_r[:, c, :], hT[:, c, :], start=c == 0, stop=c == KC - 1)
                ins.then_inc(r_mm, 1)
                pe.wait_ge(ws_in, 32)
                for f in range(2):
                    for k, w in enumerate((w_s1, w_s3)):
                        for c in range(KC):
                            ins = nc.tensor.matmul(bank[2 + 2 * f + k][:, 0:TOK], w[:, c, f:FE:2], hT[:, c, :],
                                                   start=c == 0, stop=c == KC - 1)
                        ins.then_inc(sh_mm, 1)
                    if f == 0:
                        pe.wait_ge(r_sg, 1)
                        for j in range(NT):
                            ins = nc.tensor.transpose(bank[1][:, j * E:(j + 1) * E], lgT[:, j * P:(j + 1) * P], ident[0:E, 0:E])
                        ins.then_inc(r_T, 1)
                pe.wait_ge(sh_ok, 2)
                pe.wait_ge(ws2_in, 16)
                for j in range(NT):
                    for n in range(2):
                        if 2 * j + n >= 2:
                            pe.wait_ge(sy_ok, 2 * j + n - 1)
                        for f in range(2):
                            ins = nc.tensor.matmul(bank[6 + n][:, :], hs[:, f, j * P:(j + 1) * P], w_s2[:, f, 512 * n:512 * n + 512],
                                                   start=f == 0, stop=f == 1)
                        ins.then_inc(sy_mm, 1)
                pe.wait_ge(sel_ok, 1)
                msv = by_tile(MS)
                for j in range(NT):
                    for k in range(j + 1):
                        nc.tensor.matmul(bank[0][:, j * E:(j + 1) * E], const[:, C_TRI:C_TRI + P] if k == j else const[:, C_ONE:C_ONE + P],
                                         msv[:, k], start=k == 0, stop=k == j)
                for k in range(NT):
                    ins = nc.tensor.matmul(bank[0][:, 3 * E:4 * E], const[:, C_ONE:C_ONE + P], msv[:, k], start=k == 0, stop=k == NT - 1)
                ins.then_inc(pos_mm, 1)

            @block.scalar
            def _(act):
                for f in range(FT):
                    act.wait_ge(g_T, f + 1)
                    nc.scalar.activation(gT[:, f].rearrange("p (k t) -> p t k", t=LC),
                                         bank[f % 2][:, 0:TOK].rearrange("p (t k) -> p t k", t=LC), ACT.Gelu_apprx_tanh
                                         ).then_inc(g_ok, 1)
                for f in range(FT):
                    act.wait_ge(glu_mm, f + 1)
                    if f >= 2:
                        act.wait_ge(glu_ok, f - 1)
                    nc.scalar.activation(sgl[:, f % 2], bank[6 + f % 2][:, 0:TOK], ACT.Sigmoid).then_inc(glu_sg, 1)

                for j in range(NT):
                    act.wait_ge(x2_ok, 2 * j + 2)
                    if j:
                        act.wait_ge(n2_sq, j)
                    nc.scalar.activation(at(o_U, D), X[:, j], ACT.Square,
                                         accum_out=nst[:, j:j + 1]).then_inc(n2_sq, 1)
                    act.wait_ge(n2_ms, j + 1)
                    nc.scalar.activation(nst[:, 8 + j:9 + j], nst[:, 4 + j:5 + j], ACT.Sqrt).then_inc(n2_rt, 1)
                act.wait_ge(n2_g, 1)
                for j in range(NT):
                    r = 0 if j == 0 else 1
                    for h in range(2):
                        act.wait_ge(n2_T, 2 * j + h + 1)
                        for c in range(4):
                            cc = 4 * h + c
                            ins = nc.scalar.activation(hT[:, cc, j * P:(j + 1) * P], bank[6 + h][:, c * P:(c + 1) * P],
                                                       ACT.Identity, scale=gs2[:, r, cc:cc + 1], bias=mod[:, r, 3, cc:cc + 1])
                        ins.then_inc(n2_hT, 1)
                act.wait_ge(r_mm, 1)
                nc.scalar.activation(lgT, bank[0][0:E, 0:TOK], ACT.Sigmoid).then_inc(r_sg, 1)
                for f in range(2):
                    act.wait_ge(sh_mm, 2 * f + 1)
                    nc.scalar.activation(hs[:, f], bank[2 + 2 * f][:, 0:TOK], ACT.Silu).then_inc(sh_si, 1)
                act.wait_ge(H_ok, 3)
                for j in range(NT):
                    for n in range(2):
                        act.wait_ge(sy_mm, 2 * j + n + 1)
                        nc.scalar.activation(ACC[:, j, 512 * n:512 * n + 512], bank[6 + n][:, :], ACT.Copy).then_inc(sy_ok, 1)

            @block.vector
            def _(dve):
                def step(ins):
                    n_step[0] += 1
                    ins.then_inc(dve_step, 1)
                    dve.wait_ge(dve_step, n_step[0])

                tt, ts, stt = nc.vector.tensor_tensor, nc.vector.tensor_scalar, nc.vector.scalar_tensor_tensor
                dve.wait_ge(g_ok, 6)
                for n in range(4):
                    seq, f = divmod(n, 2)
                    w, t0 = (CTX, 0) if seq == 0 else (LAT, CTX)
                    dve.wait_ge(f1_mm, n + 1)
                    nc.vector.tensor_copy(PQ[:, f, :, t0:t0 + w], bank[2 + n % 2][:, 0:2 * w].rearrange("p (x t) -> p x t", x=2)
                                          ).then_inc(f1_ok, 1)
                for f in range(2):
                    dve.wait_ge(f2_mm, f + 1)
                    nc.vector.tensor_copy(yfT[:, f], bank[4 + f][:, 0:TOK]).then_inc(f2_ok, 1)
                for f in range(FT):
                    dve.wait_ge(glu_sg, f + 1)
                    tt(AT[:, f], gT[:, f], sgl[:, f % 2], ALU.mult).then_inc(glu_ok, 1)
                dve.wait_ge(x2_in, 32)
                dve.wait_ge(pos2_in, 16)
                tt(X[:, 1:3], X[:, 1:3], pos_t, ALU.add).then_inc(xp_ok, 1)
                for m in range(KC):
                    dve.wait_ge(pr_mm, m + 1)
                    tt(GLT[:, m], GLT[:, m], bank[m % 2][:, 0:TOK], ALU.mult)
                    step(tt(GLT[:, 8 + m], GLT[:, 8 + m], bank[2 + m % 2][:, 0:TOK], ALU.mult))
                    tt(GLT[:, m], GLT[:, m], GLT[:, 8 + m], ALU.add).then_inc(pr_ok, 1)
                dve.wait_ge(bc_in, 144)
                for r in range(2):
                    stt(out=gs2[:, r], in0=mod[:, r, 4, :], scalar=1.0, in1=g2n, op0=ALU.add, op1=ALU.mult)
                    ins = stt(out=gs2b[:, r], in0=gs2b[:, r], scalar=1.0, in1=g2g_b, op0=ALU.add, op1=ALU.mult)
                ins.then_inc(n2_g, 1)
                dve.wait_ge(xp_ok, 1)
                for j in range(NT):
                    r = 0 if j == 0 else 1
                    for n in range(2):
                        cols_ = slice(512 * n, 512 * n + 512)
                        dve.wait_ge(o_mm, 2 * j + n + 1)
                        step(tt(x_new[:, n], bank[4 + n][:, :], g1b[:, r, cols_], ALU.mult))
                        tt(X[:, j, cols_], X[:, j, cols_], x_new[:, n], ALU.add).then_inc(x2_ok, 1)
                for j in range(NT):
                    r = 0 if j == 0 else 1
                    dve.wait_ge(n2_sq, j + 1)
                    ts(nst[:, 4 + j:5 + j], nst[:, j:j + 1], 1.0 / D, EPS, ALU.mult, ALU.add).then_inc(n2_ms, 1)
                    dve.wait_ge(n2_rt, j + 1)
                    step(nc.vector.reciprocal(nst[:, 12 + j:13 + j], nst[:, 8 + j:9 + j]))
                    ts(xn[:, j], X[:, j], nst[:, 12 + j:13 + j], None, ALU.mult).then_inc(n2_xn, 1)
                dve.wait_ge(n2_T, 6)
                dve.wait_ge(n2_g, 1)
                dve.wait_ge(n2_xn, 3)
                for j in range(NT):
                    r = 0 if j == 0 else 1
                    step(tt(xn[:, j], xn[:, j], gs2b[:, r], ALU.mult))
                    tt(H[:, j].rearrange("p (c q) -> p q c", c=KC), xn[:, j].rearrange("p (q c) -> p q c", c=KC),
                       sh2b[:, r].rearrange("p (q c) -> p q c", c=KC), ALU.add).then_inc(H_ok, 1)
                for f in range(2):
                    dve.wait_ge(sh_mm, 2 * f + 2)
                    dve.wait_ge(sh_si, f + 1)
                    tt(hs[:, f], hs[:, f], bank[3 + 2 * f][:, 0:TOK], ALU.mult).then_inc(sh_ok, 1)
                dve.wait_ge(r_T, 1)
                step(nc.vector.tensor_copy(sc, bank[1][:, 0:NT * E]))
                step(tt(by_tile(bi), by_tile(sc), bias_b.unsqueeze(1).to_broadcast([P, NT, E]), ALU.add))
                for g in range(NT * EG):
                    ins = nc.vector.max(mx[:, 8 * g:8 * g + 8], bi[:, EGS * g:EGS * g + EGS])
                step(ins)
                mxv = mx.rearrange("p (g k) -> p g k", k=8)
                step(tt(gsc, mxv[:, :, 0], mxv[:, :, 1], ALU.add))
                gi = gsc.rearrange("p (j g) -> p j g", j=NT).unsqueeze(3).to_broadcast([P, NT, EG, EG])
                gj = gsc.rearrange("p (j g) -> p j g", j=NT).unsqueeze(2).to_broadcast([P, NT, EG, EG])
                r4 = lambda v: v.rearrange("p (j a b) -> p j a b", j=NT, a=EG)
                low = const[:, C_LOW:C_LOW + 64].rearrange("p (a b) -> p a b", a=EG).unsqueeze(1).to_broadcast([P, NT, EG, EG])
                tt(r4(gtm), gj, gi, ALU.is_gt)
                step(tt(r4(eqm), gj, gi, ALU.is_equal))
                step(tt(r4(eqm), r4(eqm), low, ALU.mult))
                step(tt(gtm, gtm, eqm, ALU.add))
                step(nc.vector.tensor_reduce(rnk, gtm.rearrange("p (g k) -> p g k", k=EG), AX_X, ALU.add))
                step(ts(gm, rnk, float(EGK), None, ALU.is_lt))
                step(ts(gneg, gm, BIG, -BIG, ALU.mult, ALU.add))
                g8 = lambda v: v.rearrange("p (g k) -> p g k", k=EGS)
                step(tt(g8(msk), g8(bi), gm.unsqueeze(2).to_broadcast([P, NT * EG, EGS]), ALU.mult))
                step(tt(g8(msk), g8(msk), gneg.unsqueeze(2).to_broadcast([P, NT * EG, EGS]), ALU.add))
                for j in range(NT):
                    ins = nc.vector.max(th8[:, 8 * j:8 * j + 8], msk[:, E * j:E * j + E])
                step(ins)
                for j in range(NT):
                    th = th8[:, 8 * j + TOPK - 1:8 * j + TOPK]
                    ts(gtm[:, E * j:E * j + E], msk[:, E * j:E * j + E], th, None, ALU.is_gt)
                    ins = ts(eqm[:, E * j:E * j + E], msk[:, E * j:E * j + E], th, None, ALU.is_equal)
                step(ins)
                step(nc.vector.tensor_reduce(ngt, by_tile(gtm), AX_X, ALU.add))
                ts(lim, ngt, -1.0, float(TOPK), ALU.mult, ALU.add)
                for j in range(NT):
                    ins = nc.vector.tensor_tensor_scan(cum[:, E * j:E * j + E], eqm[:, E * j:E * j + E], eqm[:, E * j:E * j + E],
                                                       0.0, ALU.add, ALU.bypass)
                step(ins)
                for j in range(NT):
                    ins = stt(out=cum[:, E * j:E * j + E], in0=cum[:, E * j:E * j + E], scalar=lim[:, j:j + 1],
                              in1=eqm[:, E * j:E * j + E], op0=ALU.is_le, op1=ALU.mult)
                step(ins)
                tt(MS, gtm, cum, ALU.add).then_inc(sel_ok, 1)
                dve.wait_ge(sel_ok, 1)
                step(tt(tmpE, sc, MS, ALU.mult))
                step(nc.vector.tensor_reduce(wsum, by_tile(tmpE), AX_X, ALU.add))
                step(nc.vector.reciprocal(wrec, wsum))
                for j in range(NT):
                    ts(GT[:, E * j:E * j + E], tmpE[:, E * j:E * j + E], wrec[:, j:j + 1], SCALE, ALU.mult, ALU.mult)
                dve.wait_ge(pos_mm, 1)
                step(stt(out=posM, in0=bank[0][:, 0:NT * E], scalar=1.0, in1=MS, op0=ALU.add, op1=ALU.mult))
                ts(posM, posM, 1.0, None, ALU.subtract)
                nc.vector.tensor_copy(cnt, bank[0][:, 3 * E:4 * E]).then_inc(pos_ok, 1)

        SLOTS = BATCH * SL
        MAXT = 40
        assert MAXT >= TOK * TOPK // (SL + 1) and MAXT % BATCH == 0 and MAXT <= E
        slot = [at(o_A + 6144 * k, 6144) for k in range(RING)]
        slot13 = [v[:, 0:4096].rearrange("p (w c n) -> p w c n", w=2, c=KC) for v in slot]
        slot2 = [v[:, 4096:6144].rearrange("p (f n) -> p f n", f=2) for v in slot]
        first_stages.close()
        sb_H = ctx.enter_context(nc.sbuf_tensor("sb_H", [P, 2 * NT * D], F32R))
        sb_Y = ctx.enter_context(nc.sbuf_tensor("sb_Y", [P, 8 * D], F32R))
        sb_ST = ctx.enter_context(nc.sbuf_tensor("sb_ST", [P, 4 * TOK], F32R))
        sb_S = ctx.enter_context(nc.sbuf_tensor("sb_S", [P, NT * SLOTS], F32R))
        sb_g = ctx.enter_context(nc.sbuf_tensor("sb_g", [P, NT * 2 * BATCH], F32R))
        by_row = lambda v: v.rearrange("p (j n) -> p j n", j=NT)
        X = by_row(at(o_V, NT * D))
        g2b = at(o_A, 2 * D).rearrange("p (r n) -> p r n", r=2)
        fin_g = at(o_A + 2 * D, D)
        OUT = by_row(at(o_A + 6144, NT * D))
        Hh, Hl = [by_row(sb_H[:, 3072 * k:3072 * k + 3072]) for k in range(2)]
        slot = [at(o_A + 6144 * k, 6144) for k in range(RING)]
        slot13 = [v[:, 0:4096].rearrange("p (w c n) -> p w c n", w=2, c=KC) for v in slot]
        slot2 = [v[:, 4096:6144].rearrange("p (f n) -> p f n", f=2) for v in slot]
        XT = at(o_V, KC * SLOTS).rearrange("p (c s) -> p c s", c=KC)
        S = by_row(sb_S[:, :])
        YR = sb_Y[:, :].rearrange("p (x q n) -> p x q n", x=2, q=4)
        Y = YR.bitcast(F32)
        ST = sb_ST[:, :].rearrange("p (q t) -> p q t", q=4)
        hid = at(o_K + 1024, 512).rearrange("p (b f) -> p b f", b=2)
        silu = at(o_K + 1536, FE)
        hidT = at(o_K + 1792, 256).rearrange("p (f s) -> p f s", f=2)
        OH = at(o_K + 1024, 512)
        tmp512 = at(o_ch, 512)
        pm8, ga8 = misc[:, 384:408], misc[:, 408:432]
        gahl_r = sb_g[:, 0:48].rearrange("p (j x k) -> p j x k", j=NT, x=2)
        gahl = gahl_r.bitcast(F32)
        gcol = misc[:, 176:180]
        n_ex, cum_ex, pfx = [at(o_const + C_TRI + E * k, E) for k in range(3)]
        posr = at(o_const + C_ONE + E, E)
        ids, idx_f = misc[0:1, 432:432 + MAXT + 1].bitcast(I32), misc[0:1, 480:480 + MAXT]
        k64, five = misc[:, 520:528], misc[0:1, 472:477]
        iota = const[:, C_IOTA:C_IOTA + E]
        gate_flat = at(o_K + 2496, 256)
        pos_flat = at(o_K + 2304, 256)

        w13_in = [sem(f"w13_in{k}") for k in range(RING)]
        w2_in = [sem(f"w2_in{k}") for k in range(RING)]
        (fin_in, hh_ok, hl_ok, S_ok, ga_high, g_mm, xa, xd, h_mm, silu_ok, hid_ok, hidT_mm, hidT_ok, y0_mm, y1_mm, ya, yd, gcol_ok,
         st_mm, st_ok, sc_mm, acc_ok, pm_ok, ga_ok, tail_ok, tail_step, x3_ok, y_ready) = [sem(n) for n in (
             "fin_in", "h_high_ok", "h_low_ok", "S_ok", "ga_high", "gather_mm", "xt_act", "xt_dve", "h_mm", "silu_ok", "hid_ok", "hidT_mm",
             "hidT_ok", "y0_mm", "y1_mm", "y_high", "y_low", "gate_col_ok", "st_mm", "st_ok", "scatter_mm", "acc_ok", "pm_ok",
             "gates_ok", "tail_ok", "tail_step", "x3_ok", "y_ready")]
        NB = E // BATCH

        def wait_last(eng, s, value):
            if not isinstance(value, int) or value > 0:
                eng.wait_ge(s, value)

        def batches(eng, body):
            body(lambda per, off=0: off, BATCH)
            with eng.Fori(0, NB - 1) as b:
                body(lambda per, off=0: b * per + (per + off), b * BATCH + 2 * BATCH)
            eng.wait_ge(tail_ok, 1)
            more = eng.value_load(ids[0:1, 0:1], min_val=0, max_val=MAXT // BATCH)
            with eng.If(more > 0):
                with eng.Fori(0, more) as b:
                    body(lambda per, off=0: b * per + (NB * per + off), None)
            return more

        with nc.Block() as block:
            @block.sync
            def _(sp):
                w1 = i["w1"][0].rearrange("e (p c) n -> p e (c n)", c=KC)
                w3 = i["w3"][0].rearrange("e (p c) n -> p e (c n)", c=KC)
                w2 = i["w2"][0].rearrange("e (p c) n -> p e (c n)", c=2)

                def load13(k, e):
                    for n, w in enumerate((w1, w3)):
                        sp.dma_start(slot[k][:, 2048 * n:2048 * n + 2048], w[:, e, :]).then_inc(w13_in[k], 16)

                def load2(k, e):
                    sp.dma_start(slot[k][:, 4096:6144], w2[:, e, :]).then_inc(w2_in[k], 16)

                for k in range(RING):
                    load13(k, slice(k, k + 1))
                    load2(k, slice(k, k + 1))
                with sp.Fori(0, E // RING - 1) as g:
                    for q in range(2):
                        e = [g * RING + (RING + k) for k in (2 * q, 2 * q + 1)]
                        sp.wait_ge(h_mm, g * 2 + (q + 1))
                        for a in range(2):
                            load13(2 * q + a, bass.ds(e[a], 1))
                        sp.wait_ge(y1_mm, g * 2 + (q + 1))
                        for a in range(2):
                            load2(2 * q + a, bass.ds(e[a], 1))
                sp.wait_ge(tail_ok, 1)
                more = sp.value_load(ids[0:1, 0:1], min_val=0, max_val=MAXT // BATCH)
                with sp.If(more > 0):
                    with sp.Fori(0, more) as b:
                        for q in range(4):
                            e = [sp.value_load(ids[0:1, bass.ds(b * BATCH + (2 * q + a + 1), 1)], min_val=0, max_val=E - 1)
                                 for a in range(2)]
                            sp.wait_ge(h_mm, b * 4 + (E // 2 + q - 1))
                            for a in range(2):
                                load13((2 * q + a) % RING, bass.ds(e[a], 1))
                            sp.wait_ge(y1_mm, b * 4 + (E // 2 + q - 1))
                            for a in range(2):
                                load2((2 * q + a) % RING, bass.ds(e[a], 1))
                sp.wait_ge(h_mm, more * 4 + 4 * NB)
                sp.dma_start(X, x2_dram).then_inc(fin_in, 16)
                for r in range(2):
                    sp.dma_start(g2b[:, r, :], ada_dram[r, 5 * D:6 * D].partition_broadcast(P)).then_inc(fin_in, 16)
                sp.dma_start(fin_g, i["final_norm_g"].partition_broadcast(P)).then_inc(fin_in, 16)
                sp.wait_ge(y_ready, 1)
                sp.dma_start(o["y_prompt"][0], OUT[:, 0]).then_inc(dram_out, 16)
                sp.wait_ge(y_ready, 3)
                sp.dma_start(o["y_sample"][0].rearrange("(j p) n -> p j n", p=P), OUT[:, 1:3]).then_inc(dram_out, 16)
                sp.wait_ge(dram_out, 80)

            @block.tensor
            def _(pe):
                def body(n, following):
                    def slot_rows(p):
                        wait_last(pe, gcol_ok, n(4, p))
                        for j in range(NT):
                            nc.tensor.transpose(bank[7][:, j * P:(j + 1) * P], S[:, j, P * p:P * p + P].bitcast(F32), ident)
                        for j in range(NT):
                            ins = nc.tensor.matmul(bank[7][:, 384:400], S[:, j, P * p:P * p + P],
                                                   gahl_r[:, j].rearrange("p x k -> p (x k)"), start=j == 0, stop=j == NT - 1)
                        ins.then_inc(st_mm, 1)

                    def hidden(p):
                        if p == 0:
                            pe.wait_ge(xa, n(4, 4))
                            pe.wait_ge(xd, n(4, 4))
                        for a in range(2):
                            pe.wait_ge(w13_in[(2 * p + a) % RING], n(64, 32 * ((2 * p + a) // RING + 1)))
                        wait_last(pe, hid_ok, n(4, p - 1 if p >= 2 else 0))
                        for c in range(KC):
                            for a in range(2):
                                ins = nc.tensor.matmul(bank[2 + p % 2][64 * a:64 * a + 64, :],
                                                       XT[:, c, SL * (2 * p + a):SL * (2 * p + a + 1)],
                                                       slot13[(2 * p + a) % RING][:, :, c, :], start=c == 0, stop=c == KC - 1)
                        ins.then_inc(h_mm, 1)

                    def down(p):
                        pe.wait_ge(hid_ok, n(4, p + 1))
                        for f in range(2):
                            ins = nc.tensor.transpose(bank[4][:, f * P:(f + 1) * P], hid[:, p % 2, f:FE:2], ident)
                        ins.then_inc(hidT_mm, 1)
                        pe.wait_ge(hidT_ok, n(4, p + 1))
                        wait_last(pe, yd, n(8, 2 * p))
                        for a in range(2):
                            pe.wait_ge(w2_in[(2 * p + a) % RING], n(32, 16 * ((2 * p + a) // RING + 1)))
                        for h in range(2):
                            for f in range(2):
                                for a in range(2):
                                    ins = nc.tensor.matmul(bank[5 + h][64 * a:64 * a + 64, :], hidT[:, f, 64 * a:64 * a + 64],
                                                           slot2[(2 * p + a) % RING][:, f, 512 * h:512 * h + 512],
                                                           start=f == 0, stop=f == 1)
                            ins.then_inc((y0_mm, y1_mm)[h], 1)

                    pe.wait_ge(S_ok, n(1, 1 if following is not None else 2))
                    for c in range(KC):
                        if c < 2:
                            wait_last(pe, acc_ok, n(6))
                        else:
                            pe.wait_ge((xa, xd)[c % 2], n(4, c // 2))
                        for j in range(NT):
                            for x, part in enumerate((Hh, Hl)):
                                ins = nc.tensor.matmul(bank[c % 2][:, :], part[:, j, c * P:(c + 1) * P], S[:, j, :],
                                                       start=j == 0 and x == 0, stop=j == NT - 1 and x == 1)
                        ins.then_inc(g_mm, 1)
                    pe.wait_ge(ga_ok, n(1, 1 if following is not None else 2))
                    slot_rows(0)
                    hidden(0)
                    slot_rows(1)
                    hidden(1)
                    slot_rows(2)
                    down(0)
                    slot_rows(3)
                    hidden(2)
                    down(1)
                    hidden(3)
                    down(2)
                    down(3)
                    pe.wait_ge(st_ok, n(4, 4))
                    pe.wait_ge(yd, n(8, 8))
                    for m in range(2 * NT):
                        j, h = divmod(m, 2)
                        if m >= 2:
                            pe.wait_ge(acc_ok, n(6, m - 1))
                        for p in range(4):
                            for x in range(2):
                                ins = nc.tensor.matmul(bank[m % 2][:, :], ST[:, p, j * P:(j + 1) * P],
                                                       YR[:, x, p, 512 * h:512 * h + 512], start=p == 0 and x == 0, stop=p == 3 and x == 1)
                        ins.then_inc(sc_mm, 1)

                pe.wait_ge(hl_ok, NT)
                batches(pe, body)

            @block.scalar
            def _(act):
                def body(n, following):
                    def slot_rows(p):
                        act.wait_ge(st_mm, n(4, p + 1))
                        nc.scalar.activation(ST[:, p], bank[7][:, 0:TOK], ACT.Copy).then_inc(st_ok, 1)

                    def hidden(p):
                        act.wait_ge(h_mm, n(4, p + 1))
                        wait_last(act, hid_ok, n(4, p))
                        nc.scalar.activation(silu, bank[2 + p % 2][:, 0:FE], ACT.Silu).then_inc(silu_ok, 1)

                    def down(p):
                        act.wait_ge(hidT_mm, n(4, p + 1))
                        nc.scalar.activation(hidT.rearrange("p f s -> p (f s)"), bank[4][:, 0:2 * P], ACT.Copy).then_inc(hidT_ok, 1)
                        for h in range(2):
                            act.wait_ge((y0_mm, y1_mm)[h], n(4, p + 1))
                            nc.scalar.activation(YR[:, 0, p, 512 * h:512 * h + 512], bank[5 + h][:, :], ACT.Copy).then_inc(ya, 1)

                    for c in range(0, KC, 2):
                        act.wait_ge(g_mm, n(8, c + 1))
                        nc.scalar.activation(XT[:, c], bank[0][:, :], ACT.Copy).then_inc(xa, 1)
                    wait_last(act, sc_mm, n(6))
                    slot_rows(0)
                    hidden(0)
                    slot_rows(1)
                    hidden(1)
                    slot_rows(2)
                    down(0)
                    slot_rows(3)
                    hidden(2)
                    down(1)
                    hidden(3)
                    down(2)
                    down(3)

                for j in range(NT):
                    nc.scalar.activation(Hh[:, j], H[:, j], ACT.Copy).then_inc(hh_ok, 1)
                more = batches(act, body)
                for j in range(NT):
                    act.wait_ge(x3_ok, j + 1)
                    nc.scalar.activation(slot[2][:, j * D:(j + 1) * D], X[:, j], ACT.Square,
                                         accum_out=nst[:, j:j + 1]).then_inc(n2_sq, 1)
                    act.wait_ge(n2_ms, NT + j + 1)
                    nc.scalar.activation(nst[:, 8 + j:9 + j], nst[:, 4 + j:5 + j], ACT.Sqrt).then_inc(n2_rt, 1)

            @block.vector
            def _(dve):
                tt, ts, stt = nc.vector.tensor_tensor, nc.vector.tensor_scalar, nc.vector.scalar_tensor_tensor
                v8 = lambda v: v.rearrange("p (k s) -> p k s", k=BATCH)
                iota8 = iota.unsqueeze(1).to_broadcast([P, BATCH, SL])

                def slots(high_ready):
                    g = ga8.rearrange("p (j k) -> p j k", j=NT)
                    nc.vector.tensor_copy(gahl_r[:, :, 0], g).then_inc(ga_high, 1)
                    for j in range(NT):
                        ins = tt(v8(S[:, j]), iota8, pm8[:, 8 * j:8 * j + 8].unsqueeze(2).to_broadcast([P, BATCH, SL]),
                                 ALU.is_equal)
                    ins.then_inc(S_ok, 1)
                    dve.wait_ge(ga_high, high_ready)
                    tt(gahl_r[:, :, 1], g, gahl[:, :, 0], ALU.subtract).then_inc(ga_ok, 1)

                def pick(cols_):
                    for j in range(NT):
                        nc.vector.tensor_copy(pm8[:, 8 * j:8 * j + 8], pos_flat[:, cols_(j)])
                    for j in range(NT):
                        ins = nc.vector.tensor_copy(ga8[:, 8 * j:8 * j + 8], gate_flat[:, cols_(j)])
                    ins.then_inc(pm_ok, 1)

                def body(n, following):
                    if following is None:
                        tail_slots(n)
                    for c in range(1, KC, 2):
                        dve.wait_ge(g_mm, n(8, c + 1))
                        nc.vector.tensor_copy(XT[:, c], bank[1][:, :]).then_inc(xd, 1)

                    def gates(p):
                        dve.wait_ge(st_ok, n(4, p + 1))
                        for a in range(2):
                            r = slice(64 * a, 64 * a + 64)
                            ins = nc.vector.tensor_reduce(gcol[r, p:p + 1], gate_ps[r, :, 2 * p + a], AX_X, ALU.add)
                        ins.then_inc(gcol_ok, 1)

                    def hidden(p):
                        dve.wait_ge(silu_ok, n(4, p + 1))
                        dve.wait_ge(gcol_ok, n(4, p + 1))
                        stt(out=hid[:, p % 2], in0=silu, scalar=gcol[:, p:p + 1], in1=bank[2 + p % 2][:, FE:2 * FE],
                            op0=ALU.mult, op1=ALU.mult).then_inc(hid_ok, 1)

                    def down(p):
                        if p == 0:
                            wait_last(dve, sc_mm, n(6))
                        for h in range(2):
                            dve.wait_ge(ya, n(8, 2 * p + h + 1))
                            cols_ = slice(512 * h, 512 * h + 512)
                            tt(YR[:, 1, p, cols_], bank[5 + h][:, :], Y[:, 0, p, cols_], ALU.subtract).then_inc(yd, 1)

                    gates(0)
                    hidden(0)
                    gates(1)
                    hidden(1)
                    gates(2)
                    down(0)
                    gates(3)
                    if following is not None:
                        pick(lambda j: bass.ds(following + j * E, BATCH))
                        dve.wait_ge(pm_ok, n(1, 2))
                        slots(n(1, 2))
                    hidden(2)
                    down(1)
                    hidden(3)
                    down(2)
                    down(3)
                    for m in range(2 * NT):
                        j, h = divmod(m, 2)
                        dve.wait_ge(sc_mm, n(6, m + 1))
                        wait_last(dve, acc_ok, n(6, m))
                        tt(ACC[:, j, 512 * h:512 * h + 512], ACC[:, j, 512 * h:512 * h + 512], bank[m % 2][:, :], ALU.add
                           ).then_inc(acc_ok, 1)

                TS = 18

                def tail_slots(n):
                    count = [0]

                    def step(ins):
                        count[0] += 1
                        ins.then_inc(tail_step, 1)
                        dve.wait_ge(tail_step, n(TS, count[0] - NB * TS))

                    kb = iota[:, 0:BATCH].unsqueeze(2).to_broadcast([P, BATCH, E])
                    row = lambda v: v.unsqueeze(1).to_broadcast([P, BATCH, E])
                    oh, t8 = OH.rearrange("p (k e) -> p k e", k=BATCH), tmp512.rearrange("p (k e) -> p k e", k=BATCH)
                    dve.wait_ge(sc_mm, n(6))
                    tt(oh, kb, row(pfx), ALU.is_ge)
                    step(tt(t8, kb, row(cum_ex), ALU.is_lt))
                    step(tt(oh, oh, t8, ALU.mult))
                    for j in range(NT):
                        step(stt(out=posr, in0=pfx, scalar=float(SL), in1=pos_flat[:, j * E:j * E + E], op0=ALU.mult, op1=ALU.add))
                        step(tt(t8, oh, row(posr), ALU.mult))
                        step(nc.vector.tensor_reduce(pm8[:, 8 * j:8 * j + 8], t8, AX_X, ALU.add))
                        step(tt(t8, oh, row(GT[:, j * E:j * E + E]), ALU.mult))
                        step(nc.vector.tensor_reduce(ga8[:, 8 * j:8 * j + 8], t8, AX_X, ALU.add))
                    ts(pfx, pfx, float(BATCH), None, ALU.subtract)
                    step(ts(cum_ex, cum_ex, float(BATCH), None, ALU.subtract))
                    assert count[0] == TS, count[0]
                    for j in range(NT):
                        ins = tt(pm8[:, 8 * j:8 * j + 8], pm8[:, 8 * j:8 * j + 8], k64, ALU.subtract)
                    ins.then_inc(pm_ok, 1)
                    dve.wait_ge(pm_ok, n(1, 2))
                    dve.wait_ge(g_mm, n(8))
                    slots(n(1, 2))

                gate_ps = bank[7][:, 384:400].rearrange("p (x k) -> p x k", x=2)
                for j in range(NT):
                    dve.wait_ge(hh_ok, j + 1)
                    tt(Hl[:, j], H[:, j], Hh[:, j].bitcast(F32), ALU.subtract).then_inc(hl_ok, 1)
                pick(lambda j: slice(j * E, j * E + BATCH))
                dve.wait_ge(pm_ok, 1)
                slots(1)
                def step(ins):
                    n_step[0] += 1
                    ins.then_inc(dve_step, 1)
                    dve.wait_ge(dve_step, n_step[0])

                step(ts(n_ex, cnt, float(SL), None, ALU.is_gt))
                for r in range(2, TOK // SL):
                    step(stt(out=n_ex, in0=cnt, scalar=float(SL * r), in1=n_ex, op0=ALU.is_gt, op1=ALU.add))
                step(nc.vector.tensor_tensor_scan(cum_ex, n_ex, n_ex, 0.0, ALU.add, ALU.bypass))
                ts(k64, iota[:, 0:BATCH], float(SL), float(SL), ALU.mult, ALU.add)
                step(tt(pfx, cum_ex, n_ex, ALU.subtract))
                row1 = lambda v: v[0:1].unsqueeze(1).to_broadcast([1, BATCH, E])
                who, below = [v[0:1].rearrange("p (k e) -> p k e", k=BATCH) for v in (OH, tmp512)]
                for m in range(0, MAXT, BATCH):
                    item = iota[0:1, m:m + BATCH].unsqueeze(2).to_broadcast([1, BATCH, E])
                    tt(who, item, row1(pfx), ALU.is_ge)
                    step(tt(below, item, row1(cum_ex), ALU.is_lt))
                    step(tt(who, who, below, ALU.mult))
                    step(tt(who, who, row1(iota), ALU.mult))
                    step(nc.vector.tensor_reduce(idx_f[:, m:m + BATCH], who, AX_X, ALU.add))
                step(ts(five, iota[0:1, 0:5], float(BATCH), cum_ex[0:1, E - 1:E], ALU.mult, ALU.is_lt))
                step(nc.vector.tensor_reduce(misc[0:1, 478:479], five, AX_X, ALU.add))
                nc.vector.tensor_copy(ids[:, 1:1 + MAXT], idx_f)
                nc.vector.tensor_copy(ids[:, 0:1], misc[0:1, 478:479]).then_inc(tail_ok, 1)

                more = batches(dve, body)
                dve.wait_ge(acc_ok, more * 6 + 6 * NB)
                dve.wait_ge(fin_in, 64)
                for j in range(NT):
                    r = 0 if j == 0 else 1
                    step(tt(ACC[:, j], ACC[:, j], g2b[:, r], ALU.mult))
                    tt(X[:, j], X[:, j], ACC[:, j], ALU.add).then_inc(x3_ok, 1)
                dve.wait_ge(x3_ok, 3)
                for j in range(NT):
                    dve.wait_ge(n2_sq, NT + j + 1)
                    ts(nst[:, 4 + j:5 + j], nst[:, j:j + 1], 1.0 / D, EPS, ALU.mult, ALU.add).then_inc(n2_ms, 1)
                    dve.wait_ge(n2_rt, NT + j + 1)
                    step(nc.vector.reciprocal(nst[:, 12 + j:13 + j], nst[:, 8 + j:9 + j]))
                    stt(out=OUT[:, j], in0=X[:, j], scalar=nst[:, 12 + j:13 + j], in1=fin_g, op0=ALU.mult, op1=ALU.mult
                        ).then_inc(y_ready, 1)


_INS = ("x_prompt", "x_sample", "state_s5_re", "state_s5_im", "c", "c_ctx", "w_ada", "b_ada", "norm1_g", "norm2_g",
        "w_in", "lam_re", "lam_im", "log_dt", "b_re", "b_im", "c_re", "c_im", "d_skip", "w_glu", "w_proj_s5", "w_proj_f",
        "w_out", "w_router", "router_bias", "w1", "w3", "w2", "ws1", "ws3", "ws2", "final_norm_g")


def kernel(**inputs):
    import concourse.bacc as bacc
    from concourse.bass_utils import run_bass_kernel_spmd

    nc = bacc.Bacc("TRN2", target_bir_lowering=False, num_devices=1)
    arrays = {name: np.ascontiguousarray(inputs[name]) for name in _INS}
    arrays.update(zip(("k_const", "k_dft", "k_pos"), shape_constants()))
    i = {name: nc.dram_tensor(name, a.shape, mybir.dt.from_np(a.dtype), kind="ExternalInput").ap() for name, a in arrays.items()}
    o = {name: nc.dram_tensor(name, shape, F32, kind="ExternalOutput").ap() for name, shape in OUTS.items()}
    build(nc, i, o)
    r = run_bass_kernel_spmd(nc, [arrays], core_ids=[0])
    return tuple(r.results[0][name] for name in OUTS)
```
